# Optimizing a Trainium2 kernel written in Bass

```python
import jax
import jax.numpy as jnp
from jax import lax
import numpy as np

D_MODEL = 1024
BATCH = 1
SEQ = 512
DEPTH = 2
DEC_BATCH = 8
DEC_SEQ = 1
PAST_LEN = 2048
PAGE_SIZE = 128

N_BRANCH = 4
BRANCH_WIDTH = D_MODEL // 2
SC_CONV_W = 3
CF_CONV_W = 31
N_HEADS = 8
N_KV_HEADS = 2
HEAD_DIM = 64
GROUP = N_HEADS // N_KV_HEADS
WINDOW = 128
ATTN_BLOCK = 128
ROPE_THETA = 10000.0
GLA_HEADS = 4
GLA_DK = 64
GLA_DV = BRANCH_WIDTH // GLA_HEADS
GLA_GATE_RANK = 16
GLA_GATE_NORM = 16.0
GLA_CHUNK = 64
D_FF = -(-8 * D_MODEL // (3 * 256)) * 256
NEG_INF = -1e30
RMS_EPS = 1e-6
LN_EPS = 1e-5

IN_SPLITS = (BRANCH_WIDTH, BRANCH_WIDTH, BRANCH_WIDTH,
             BRANCH_WIDTH, BRANCH_WIDTH,
             N_HEADS * HEAD_DIM, N_KV_HEADS * HEAD_DIM, N_KV_HEADS * HEAD_DIM,
             GLA_HEADS * GLA_DK, GLA_HEADS * GLA_DK, GLA_HEADS * GLA_DV,
             GLA_HEADS * GLA_DV, GLA_GATE_RANK,
             N_BRANCH * D_MODEL)
IN_WIDTH = sum(IN_SPLITS)
IN_SPLIT_POINTS = tuple(int(s) for s in np.cumsum(IN_SPLITS)[:-1])

kernel_name = 'hybrid_gated_branch_decoder_step'

def rms_norm(x, g):
    xf = x.astype(jnp.float32)
    y = xf * lax.rsqrt(jnp.mean(xf * xf, axis=-1, keepdims=True) + RMS_EPS)
    return (y * g.astype(jnp.float32)).astype(x.dtype)

def layer_norm(x, g, b):
    xf = x.astype(jnp.float32)
    mu = jnp.mean(xf, axis=-1, keepdims=True)
    xc = xf - mu
    y = xc * lax.rsqrt(jnp.mean(xc * xc, axis=-1, keepdims=True) + LN_EPS)
    return (y * g.astype(jnp.float32) + b.astype(jnp.float32)).astype(x.dtype)

def rope(x, pos):
    half = HEAD_DIM // 2
    inv = ROPE_THETA ** (-jnp.arange(half, dtype=jnp.float32) / half)
    ang = pos.astype(jnp.float32)[:, None] * inv[None, :]
    cos = jnp.cos(ang)[None, :, None, :]
    sin = jnp.sin(ang)[None, :, None, :]
    xf = x.astype(jnp.float32)
    x1, x2 = xf[..., :half], xf[..., half:]
    return jnp.concatenate([x1 * cos - x2 * sin, x2 * cos + x1 * sin], axis=-1).astype(x.dtype)

def causal_dwconv(buf, u, w, b=None):
    width = w.shape[0]
    ucat = jnp.concatenate([buf.astype(u.dtype), u], axis=1)
    y = lax.conv_general_dilated(ucat, w[:, None, :].astype(u.dtype), window_strides=(1,), padding='VALID',
                                 dimension_numbers=('NWC', 'WIO', 'NWC'), feature_group_count=u.shape[-1])
    if b is not None:
        y = y + b
    return y, ucat[:, ucat.shape[1] - (width - 1):]

def sliding_window_attention(q, k, v, k_buf, v_buf, start, sinks):
    B, L = q.shape[0], q.shape[1]
    W = k_buf.shape[1]
    qb_size = min(ATTN_BLOCK, L)
    nb = -(-L // qb_size)
    Lp = nb * qb_size
    pad = ((0, 0), (0, Lp - L), (0, 0), (0, 0))
    new_k_buf = jnp.concatenate([k_buf, k], axis=1)[:, -WINDOW:]
    new_v_buf = jnp.concatenate([v_buf, v], axis=1)[:, -WINDOW:]
    k_all = jnp.concatenate([k_buf, jnp.pad(k, pad)], axis=1)
    v_all = jnp.concatenate([v_buf, jnp.pad(v, pad)], axis=1)
    idx = (jnp.arange(nb) * qb_size)[:, None] + jnp.arange(qb_size + W)[None, :]
    kb = k_all[:, idx]
    vb = v_all[:, idx]
    qb = jnp.pad(q, pad).reshape(B, nb, qb_size, N_KV_HEADS, GROUP, HEAD_DIM)
    s = jnp.einsum('bnqkgd,bnskd->bnkgqs', qb, kb, preferred_element_type=jnp.float32) * (HEAD_DIM ** -0.5)
    qpos = start + jnp.arange(Lp).reshape(nb, qb_size)
    kpos = start - W + idx
    delta = qpos[:, :, None] - kpos[:, None, :]
    valid = (delta >= 0) & (delta < WINDOW) & (kpos[:, None, :] >= 0)
    s = jnp.where(valid[None, :, None, None], s, NEG_INF)
    sink = sinks.astype(jnp.float32).reshape(1, 1, N_KV_HEADS, GROUP, 1)
    m = jnp.maximum(jnp.max(s, axis=-1), sink)
    p = jnp.exp(s - m[..., None])
    denom = jnp.sum(p, axis=-1) + jnp.exp(sink - m)
    p = (p / denom[..., None]).astype(v.dtype)
    o = jnp.einsum('bnkgqs,bnskd->bnqkgd', p, vb).reshape(B, Lp, N_HEADS * HEAD_DIM)[:, :L]
    return o, new_k_buf, new_v_buf

def gla_recurrence(q, k, v, log_a, S0):
    B, L = q.shape[0], q.shape[1]
    C = min(GLA_CHUNK, L)
    n = -(-L // C)
    Lp = n * C
    pad = ((0, 0), (0, Lp - L), (0, 0), (0, 0))
    f32 = jnp.float32
    qf = jnp.pad(q.astype(f32) * (GLA_DK ** -0.5), pad).reshape(B, n, C, GLA_HEADS, GLA_DK)
    kf = jnp.pad(k.astype(f32), pad).reshape(B, n, C, GLA_HEADS, GLA_DK)
    vf = jnp.pad(v.astype(f32), pad).reshape(B, n, C, GLA_HEADS, GLA_DV)
    la = jnp.pad(log_a.astype(f32), pad).reshape(B, n, C, GLA_HEADS, GLA_DK)
    bcum = jnp.cumsum(la, axis=2)
    b_last = bcum[:, :, -1:]
    qe = qf * jnp.exp(bcum)
    ke = kf * jnp.exp(-bcum)
    kd = kf * jnp.exp(b_last - bcum)
    causal = jnp.tril(jnp.ones((C, C), dtype=bool))
    A = jnp.where(causal, jnp.einsum('bnthd,bnshd->bnhts', qe, ke), 0.0)
    o_intra = jnp.einsum('bnhts,bnshv->bnthv', A, vf)
    decay = jnp.exp(b_last[:, :, 0])

    def step(S, inp):
        qe_c, kd_c, v_c, dec_c = inp
        o_c = jnp.einsum('bthd,bhdv->bthv', qe_c, S)
        S = dec_c[..., None] * S + jnp.einsum('bthd,bthv->bhdv', kd_c, v_c)
        return S, o_c

    xs = (jnp.moveaxis(qe, 1, 0), jnp.moveaxis(kd, 1, 0), jnp.moveaxis(vf, 1, 0), jnp.moveaxis(decay, 1, 0))
    S, o_inter = lax.scan(step, S0.astype(f32), xs)
    o = o_intra + jnp.moveaxis(o_inter, 0, 1)
    return o.reshape(B, Lp, GLA_HEADS, GLA_DV)[:, :L], S

def trunk_layer(x, start, sc_buf, cf_buf, k_buf, v_buf, gla_state,
                norm_mix, w_in, conv_short, conv_conf, conv_conf_b, conf_ln_g, conf_ln_b,
                q_norm, k_norm, attn_sinks, w_gla_gate, b_gla_gate, gla_norm, w_branch, w_out,
                norm_ffn, w_ffn_in, w_ffn_out):
    B, L, _ = x.shape
    dt = x.dtype
    xn = rms_norm(x, norm_mix)
    proj = xn @ w_in
    (sc_h, sc_b, sc_c, cf_a, cf_b, aq, ak, av, gq, gk, gv, gg, ga, gates) = jnp.split(proj, IN_SPLIT_POINTS, axis=-1)
    conv_u, new_sc = causal_dwconv(sc_buf, sc_c * sc_h, conv_short)
    o_a = sc_b * conv_u
    c, new_cf = causal_dwconv(cf_buf, cf_a * jax.nn.sigmoid(cf_b), conv_conf, conv_conf_b)
    o_b = jax.nn.silu(layer_norm(c, conf_ln_g, conf_ln_b))
    pos = start + jnp.arange(L)
    q = rope(rms_norm(aq.reshape(B, L, N_HEADS, HEAD_DIM), q_norm), pos)
    k = rope(rms_norm(ak.reshape(B, L, N_KV_HEADS, HEAD_DIM), k_norm), pos)
    v = av.reshape(B, L, N_KV_HEADS, HEAD_DIM)
    o_c, new_k, new_v = sliding_window_attention(q, k, v, k_buf.astype(dt), v_buf.astype(dt), start, attn_sinks)
    log_a = jax.nn.log_sigmoid((ga @ w_gla_gate + b_gla_gate).astype(jnp.float32)) / GLA_GATE_NORM
    o_d, new_S = gla_recurrence(gq.reshape(B, L, GLA_HEADS, GLA_DK), gk.reshape(B, L, GLA_HEADS, GLA_DK),
                                gv.reshape(B, L, GLA_HEADS, GLA_DV), log_a.reshape(B, L, GLA_HEADS, GLA_DK), gla_state)
    o_d = (rms_norm(o_d.astype(dt), gla_norm) * jax.nn.silu(gg.reshape(B, L, GLA_HEADS, GLA_DV))).reshape(B, L, BRANCH_WIDTH)
    branches = jnp.stack([o_a, o_b, o_c, o_d], axis=2)
    branch_d = jnp.einsum('blrc,rcd->blrd', branches, w_branch)
    g = jax.nn.sigmoid(gates.reshape(B, L, N_BRANCH, D_MODEL))
    merged = jnp.einsum('blrd,blrd->bld', g, branch_d)
    x = x + merged @ w_out
    hu = rms_norm(x, norm_ffn) @ w_ffn_in
    h_gate, h_up = jnp.split(hu, 2, axis=-1)
    x = x + (jax.nn.silu(h_gate) * h_up) @ w_ffn_out
    return x, new_sc, new_cf, new_k, new_v, new_S.astype(dt)

def setup_inputs(seed: int = 0) -> dict:
    key = jax.random.key(seed)
    ks = jax.random.split(key, 25)
    f32 = jnp.float32

    def nrm(k, shape, scale):
        return scale * jax.random.normal(k, shape, f32)

    def gain(k, shape):
        return 1.0 + 0.02 * jax.random.normal(k, shape, f32)

    win_buf = min(WINDOW, PAST_LEN)
    return {
        'x_prompt': nrm(ks[0], (BATCH, SEQ, D_MODEL), 1.0),
        'x_sample': nrm(ks[1], (DEC_BATCH, DEC_SEQ, D_MODEL), 1.0),
        'cache_swa_k': nrm(ks[2], (DEPTH, DEC_BATCH, win_buf, N_KV_HEADS, HEAD_DIM), 1.0),
        'cache_swa_v': nrm(ks[3], (DEPTH, DEC_BATCH, win_buf, N_KV_HEADS, HEAD_DIM), 1.0),
        'state_sconv': nrm(ks[4], (DEPTH, DEC_BATCH, SC_CONV_W - 1, BRANCH_WIDTH), 1.0),
        'state_cconv': nrm(ks[5], (DEPTH, DEC_BATCH, CF_CONV_W - 1, BRANCH_WIDTH), 0.5),
        'state_gla': nrm(ks[6], (DEPTH, DEC_BATCH, GLA_HEADS, GLA_DK, GLA_DV), 1.0),
        'norm_mix': gain(ks[7], (DEPTH, D_MODEL)),
        'w_in': nrm(ks[8], (DEPTH, D_MODEL, IN_WIDTH), D_MODEL ** -0.5),
        'conv_short': nrm(ks[9], (DEPTH, SC_CONV_W, BRANCH_WIDTH), SC_CONV_W ** -0.5),
        'conv_conf': nrm(ks[10], (DEPTH, CF_CONV_W, BRANCH_WIDTH), CF_CONV_W ** -0.5),
        'conv_conf_b': nrm(ks[11], (DEPTH, BRANCH_WIDTH), 0.02),
        'conf_ln_g': gain(ks[12], (DEPTH, BRANCH_WIDTH)),
        'conf_ln_b': nrm(ks[13], (DEPTH, BRANCH_WIDTH), 0.02),
        'q_norm': gain(ks[14], (DEPTH, HEAD_DIM)),
        'k_norm': gain(ks[15], (DEPTH, HEAD_DIM)),
        'attn_sinks': nrm(ks[16], (DEPTH, N_HEADS), 0.5),
        'w_gla_gate': nrm(ks[17], (DEPTH, GLA_GATE_RANK, GLA_HEADS * GLA_DK), GLA_GATE_RANK ** -0.5),
        'b_gla_gate': nrm(ks[18], (DEPTH, GLA_HEADS * GLA_DK), 0.1),
        'gla_norm': gain(ks[19], (DEPTH, GLA_DV)),
        'w_branch': nrm(ks[20], (DEPTH, N_BRANCH, BRANCH_WIDTH, D_MODEL), BRANCH_WIDTH ** -0.5),
        'w_out': nrm(ks[21], (DEPTH, D_MODEL, D_MODEL), D_MODEL ** -0.5),
        'norm_ffn': gain(ks[22], (DEPTH, D_MODEL)),
        'w_ffn_in': nrm(ks[23], (DEPTH, D_MODEL, 2 * D_FF), D_MODEL ** -0.5),
        'w_ffn_out': nrm(ks[24], (DEPTH, D_FF, D_MODEL), D_FF ** -0.5),
    }

def reference(x_prompt, x_sample, cache_swa_k, cache_swa_v, state_sconv, state_cconv, state_gla,
              norm_mix, w_in, conv_short, conv_conf, conv_conf_b, conf_ln_g, conf_ln_b,
              q_norm, k_norm, attn_sinks, w_gla_gate, b_gla_gate, gla_norm, w_branch, w_out,
              norm_ffn, w_ffn_in, w_ffn_out):
    dt = x_prompt.dtype
    bp = x_prompt.shape[0]
    zero_sc = jnp.zeros((bp, SC_CONV_W - 1, BRANCH_WIDTH), dt)
    zero_cf = jnp.zeros((bp, CF_CONV_W - 1, BRANCH_WIDTH), dt)
    zero_kv = jnp.zeros((bp, WINDOW, N_KV_HEADS, HEAD_DIM), dt)
    zero_S = jnp.zeros((bp, GLA_HEADS, GLA_DK, GLA_DV), dt)
    yp, ys = x_prompt, x_sample
    sc_p, cf_p, k_p, v_p, S_p = [], [], [], [], []
    sc_s, cf_s, k_s, v_s, S_s = [], [], [], [], []
    for l in range(DEPTH):
        w = (norm_mix[l], w_in[l], conv_short[l], conv_conf[l], conv_conf_b[l], conf_ln_g[l], conf_ln_b[l],
             q_norm[l], k_norm[l], attn_sinks[l], w_gla_gate[l], b_gla_gate[l], gla_norm[l], w_branch[l], w_out[l],
             norm_ffn[l], w_ffn_in[l], w_ffn_out[l])
        yp, a1, a2, a3, a4, a5 = trunk_layer(yp, 0, zero_sc, zero_cf, zero_kv, zero_kv, zero_S, *w)
        sc_p.append(a1); cf_p.append(a2); k_p.append(a3); v_p.append(a4); S_p.append(a5)
        ys, b1, b2, b3, b4, b5 = trunk_layer(ys, PAST_LEN, state_sconv[l], state_cconv[l], cache_swa_k[l],
                                             cache_swa_v[l], state_gla[l], *w)
        sc_s.append(b1); cf_s.append(b2); k_s.append(b3); v_s.append(b4); S_s.append(b5)
    return (yp, ys,
            jnp.stack(sc_p), jnp.stack(sc_s),
            jnp.stack(cf_p), jnp.stack(cf_s),
            jnp.stack(k_p), jnp.stack(k_s),
            jnp.stack(v_p), jnp.stack(v_s),
            jnp.stack(S_p), jnp.stack(S_s))


_drawn_inputs = setup_inputs


def setup_inputs(seed=0):
    import zlib

    import numpy as np

    out = dict(_drawn_inputs(seed))
    spreads = {}
    factors = {'conv_conf_b': 3.066,
     'conf_ln_g': 5.463,
     'conf_ln_b': 6.088,
     'q_norm': 8.0,
     'k_norm': 2.798,
     'attn_sinks': 64.0,
     'gla_norm': 6.8,
     'norm_ffn': 2.971}
    for name, (base, spread) in spreads.items():
        noise = np.random.default_rng([zlib.crc32(name.encode()), seed]).standard_normal(out[name].shape)
        drawn = base * np.exp(spread * noise) if base else spread * noise
        out[name] = jnp.asarray(drawn.astype(out[name].dtype))
    for name, factor in factors.items():
        out[name] = (out[name] * factor).astype(out[name].dtype)
    return out
```

```python
from contextlib import ExitStack

import numpy as np

import concourse.bass as bass
from concourse import mybir

F32 = mybir.dt.float32
F32R = mybir.dt.float32r
U32 = mybir.dt.uint32
ALU = mybir.AluOpType
ACT = mybir.ActivationFunctionType
AX = mybir.AxisListType.X

P = 128
D_MODEL = 1024
SEQ = 512
DEPTH = 2
NS = 8
T = SEQ + NS
TH = T // 2
BW = 512
KD = D_MODEL // P
KB = BW // P
HEAD = 64
GROUP = 4
NKV = 2
WIN = 128
NQ = NS * NKV * GROUP
CHUNK = 64
NCHUNK = SEQ // CHUNK
NBLK = SEQ // P
D_FF = 2816
FC = D_FF // P
FA = 12
FB = FC - FA
W1, W2 = 3, 31
RMS_EPS, LN_EPS = 1e-6, 1e-5
NEG = -1e30

C_SCH, C_SCB, C_SCC, C_CFA, C_CFB = 0, 512, 1024, 1536, 2048
C_AQ, C_AK, C_AV, C_GQ, C_GK, C_GV, C_GG, C_GA, C_GATE = 2560, 3072, 3200, 3328, 3584, 3840, 4352, 4864, 4880

SLOTS = []


def _add(kind, *chunks):
    for c in chunks:
        SLOTS.append((kind, c))


for _p in (0, 2):
    _add("cfb", _p, _p + 1)
    _add("cfa", _p, _p + 1)
_add("aq", 0, 1, 2, 3)
_add("ak", 0)
_add("av", 0)
for _p in (0, 2):
    _add("sch", _p, _p + 1)
    _add("scc", _p, _p + 1)
    _add("scb", _p, _p + 1)


def _gate_steps(r):
    for half in range(2):
        _add(("gate", r), *range(4 * half, 4 * half + 4))
        _add(("branch", r), *range(4 * half, 4 * half + 4))


_gate_steps(0)
_add("gq", 0, 1)
_add("gk", 0, 1)
_add("gv", 0, 1, 2, 3)
_add("ga", 0)
_add("gg", 0, 1, 2, 3)
_gate_steps(2)
_gate_steps(1)
_gate_steps(3)
NSLOT = len(SLOTS)
FIRST = {}
for _n, _k in enumerate(SLOTS):
    FIRST.setdefault(_k[0], _n)
S_AQ, S_AV, S_SCH, S_GATE_A, S_GA, S_GATE_B = (FIRST[k] for k in ("aq", "av", "sch", ("gate", 0), "ga", ("gate", 1)))

TILE_OF = []
_t = 0
for _kind, _c in SLOTS:
    if isinstance(_kind, tuple) and _kind[0] == "branch":
        TILE_OF.append(([_t], (_c % 2) * KB * P))
        _t += _c % 2
    elif _kind == "ga":
        TILE_OF.append(([_t, _t + 1], 0))
        _t += 2
    else:
        TILE_OF.append(([_t], 0))
        _t += 1
TILES_MIX = _t
TILE_LEN = [1024] * TILES_MIX
for _t in TILE_OF[S_GA][0]:
    TILE_LEN[_t] = 512
LAST_USE = {t: n for n, (ts, _) in enumerate(TILE_OF) for t in ts}
TILE_LEN += [1024] * 2


def last_tile(n):
    return TILE_OF[min(n, NSLOT - 1)][0][-1] + (n + 2 >= NSLOT) + (n + 1 >= NSLOT)


UNITS_MIX = TILES_MIX // 2
UNITS_O = KD // 2
UNITS = UNITS_MIX + UNITS_O + FA + KD + FB + KD
N_O = NSLOT
N_F1A = N_O + KD
N_F2A = N_F1A + 2 * FA
N_F1B = N_F2A + KD
N_F2B = N_F1B + 2 * FB
T_O = TILES_MIX
T_F1A = T_O + KD
T_F2A = T_F1A + 2 * FA
T_F1B = T_F2A + 2 * KD
T_F2B = T_F1B + 2 * FB

ATT = [S_AV + n for n in (7, 9, 11, 13, 19, 21, 24, 28)]
SATT = S_AV + 4
G_VT, G_Z, G_KDT, G_U = S_GA + 1, S_GA + 3, S_GA + 9, S_GA + 13
LN_CONV, LN_SUM, LN_XC, LN_VAR, LN_Y = S_GA - 3, S_GA + 7, S_GA + 8, S_GA + 11, S_GA + 13
G_A = [S_GA + n for n in (15, 19, 21, 23)]
G_S = [S_GA + 26, S_GA + 28]
G_N = S_GA + 30

LO_FIRST = (*range(S_GA + 5, S_GA + 8), *range(G_N, G_N + 6))

TAPS = [(c, w) for w in range(W2) for c in (0, 1)] + [(2, w) for w in range(W2)]
TAPS_AT = {}
_left = len(TAPS)
for _first, _last, _m in ((4, 7, 3), (8, 9, 4), (10, 17, 2), (20, 21, 2), (29, 29, 2), (30, 33, 1), (34, 37, 2),
                          (38, 41, 1), (42, 53, 3)):
    for _n in range(_first, _last + 1):
        TAPS_AT[_n] = min(_m, _left)
        _left -= TAPS_AT[_n]
assert _left == 0, _left

PAR = {}
_at = 0
for _name, _w in (("gffn", KD), ("cs", KB * W1), ("cc", KB * W2), ("ccb", KB), ("lng", KB), ("lnb", KB),
                  ("qn", 1), ("kn", 1), ("sink", NKV * GROUP), ("sink64", 1), ("bg", 2), ("gn", 1), ("wg", 2 * P)):
    PAR[_name] = (_at, _at + _w)
    _at += _w
NPAR = _at
CST = {}
_at = 0
for _name, _w in (("cos", T), ("sin", T), ("amask", 2 * P), ("ident", P), ("ones", P), ("ones64", P), ("rot", P),
                  ("eye8", NS)):
    CST[_name] = (_at, _at + _w)
    _at += _w
NCST = _at


def constants():
    c = np.zeros((P, NCST), np.float32)
    half = HEAD // 2
    inv = np.float32(10000.0) ** (-np.arange(half, dtype=np.float32) / np.float32(half))
    pos = np.concatenate([np.arange(SEQ), np.full(NS, 2048)]).astype(np.float32)
    ang = (pos[:, None] * inv[None, :]).astype(np.float32)
    ang = np.tile(ang.T, (4, 1))
    q = np.arange(P)

    def put(name, v):
        a, b = CST[name]
        c[:v.shape[0], a:b] = v
    put("cos", np.cos(ang))
    put("sin", np.sin(ang))
    key = np.arange(2 * P)
    put("amask", np.where((key[None, :] > q[:, None]) & (key[None, :] <= q[:, None] + P), 0.0, NEG))
    put("ident", np.eye(P))
    put("ones", np.ones((P, P)))
    put("ones64", (q[:, None] // HEAD == q[None, :] // HEAD).astype(np.float32))
    rot = np.zeros((P, P))
    for m in range(P):
        if m % HEAD < half:
            rot[m + half, m] = -1.0
        else:
            rot[m - half, m] = 1.0
    put("rot", rot)
    put("eye8", np.eye(NS))
    s, t = q[:, None], q[None, :]
    glam = ((s // CHUNK == t // CHUNK) & (s <= t)).astype(np.uint32)
    tt = np.arange(T)
    scanm = np.tile(((tt % CHUNK != 0) & (tt < SEQ)).astype(np.float32), (P, 1))
    return c, glam, scanm


def build(nc, wt, xt, gm, par, cst, glam_d, scan_d, kc, vc, scst, ccst, gst,
          yt, o_sc, o_scs, o_cc, o_ccs, o_k, o_ks, o_v, o_vs, o_g, o_gs):
    ctx = ExitStack()
    with ctx:
        at = [2048]

        def place(name, shape, dt=F32, offset=None):
            size = int(np.prod(shape[1:])) * mybir.dt.size(dt)
            off = at[0] if offset is None else offset
            if offset is None:
                at[0] += (size + 31) // 32 * 32
            return nc.alloc_sbuf_tensor_at(name, list(shape), dt, offset=off)

        SL = T * 4
        raw = place("raw", [P, 2, 2048])
        whi = place("whi", [P, 4, 1024], F32R)
        wlo = place("wlo", [P, 4, 1024], F32R)
        xhi = place("xhi", [P, KD, T], F32R)
        xlo = place("xlo", [P, KD, T], F32R)
        rstd = place("rstd", [P, T])
        cs = place("cs", [P, NCST])
        glam = place("glam", [P, P], U32)
        scanm = place("scanm", [P, T], F32)
        pr = place("pr", [P, NPAR])
        gmix = place("gmix", [P, KD])
        small = place("small", [P, 336])
        tmp = place("tmp", [P, 3, T])
        ssum = place("ssum", [P, T])
        base = at[0]
        x = place("x", [P, KD, T])
        prob = place("prob", [P, GROUP, 2 * P], offset=base)
        probt = place("probt", [P, 2, GROUP * P], offset=base + 2 * SL)
        sprob = place("sprob", [NQ, P], offset=base + 4 * SL)
        qz = place("qz", [P, NS, NQ + NQ // NS], offset=base + 4 * SL + P * 4)
        vs = place("vs", [P, NS, P], offset=base + 6 * SL)
        gv = place("gv", [P, 4, T], offset=base)
        vtok = place("vtok", [P, NBLK, 4 * P], offset=base + 4 * SL)
        cfu_at = at[0]
        cfu = place("cfu", [P, KB, W2 - 1 + SEQ])
        gqz = place("gqz", [P, 2, NS, 2 * NS + 2], offset=cfu_at + NS * P * 4)
        cacc = place("cacc", [P, KB, T])
        cfs = place("cfs", [P, KB, NS, W2])
        base = at[0]
        at[0] += 12 * SL
        q = place("q", [P, GROUP, T], offset=base)
        kt = place("kt", [P, T], offset=base + 4 * SL)
        vt = place("vt", [P, T], offset=base + 5 * SL)
        vb = place("vb", [P, NBLK, P], offset=base + 6 * SL)
        kts = place("kts", [P, NS, P], offset=base + 7 * SL)
        sh = place("sh", [P, NCHUNK, 2, P], offset=base)
        gq = place("gq", [P, 2, T], offset=base + 4 * SL)
        s0 = [place("s0", [P, NS, P], offset=base + 6 * SL), place("s1", [P, NS, P], offset=cfu_at)]
        gg = place("gg", [P, 4, T], offset=base + 8 * SL)
        mlo = place("mlo", [P, KD, T], F32R, offset=base)
        base = at[0]
        at[0] += 24 * SL
        ohi = [place(f"ohi{i}", [P, KB, T], F32R, offset=base + 8 * i * SL) for i in range(2)]
        olo = [place(f"olo{i}", [P, KB, T], F32R, offset=base + (8 * i + 4) * SL) for i in range(2)]
        gk = place("gk", [P, 2, T], offset=base)
        gb = place("gb", [P, 2, T], offset=base + 2 * SL)
        kdt = place("kdt", [P, NBLK, 2 * P], offset=base + 4 * SL)
        am = place("am", [P, 4, P], offset=base + 6 * SL)
        ge = place("ge", [P, T], offset=base + 7 * SL)
        vbd = [place("vbd0", [NS, NS, P], offset=base + 4 * SL), place("vbd1", [NS, NS, P], offset=base)]
        vst = place("vst", [NS, 4 * P], offset=base + 7 * SL)
        mhi = place("mhi", [P, KD, T], F32R, offset=base + 8 * SL)
        mg = place("mg", [P, KD, T], offset=base + 16 * SL)
        scu = place("scu", [P, KB, W1 - 1 + SEQ], offset=base + 16 * SL)
        sct = place("sct", [P, 3, T], offset=base + 16 * SL + (4 * (W1 - 1 + SEQ) * 4 + 31) // 32 * 32)
        hhi = place("hhi", [P, FA, T], F32R, offset=base)
        hlo = place("hlo", [P, FA, T], F32R, offset=base + FA * SL)
        gt = place("gt", [P, 4, T])
        kds = tmp[0:NS, 2, 0:2 * P]

        def sm(a, b, rows=P):
            return small[0:rows, a:b]
        rmax, nmax, lsum, esink, rl = sm(0, 4), sm(4, 8), sm(8, 12), sm(12, 16), sm(16, 20)
        smax, slsum, sesink, srl, snmax = (sm(20 + i, 21 + i, NQ) for i in range(5))
        gdec = [sm(52 + 8 * p, 60 + 8 * p) for p in range(2)]
        gdecs = [sm(68 + 8 * p, 76 + 8 * p) for p in range(2)]
        o16 = sm(112, 240, 2 * NS)
        pts = small[:, 176:240].rearrange("p (b h) -> p b h", b=NS)
        scs = small[:, 240:336].rearrange("p (c b w) -> p c b w", c=KB, b=NS)
        vnew = tmp[0:NS, 2, 384:512]

        def cst_(name, rows=P):
            a, b = CST[name]
            return cs[0:rows, a:b]

        def par_(name, i=0, n=1, rows=P):
            a = PAR[name][0] + i
            return pr[0:rows, a:a + n]
        cosm, sinm, ident, ones = cst_("cos"), cst_("sin"), cst_("ident"), cst_("ones")

        acc = ctx.enter_context(nc.psum_tensor("acc", [P, 2, 2, 512], F32))
        m4 = ctx.enter_context(nc.psum_tensor("m4", [P, 4, 512], F32))

        def acc_of(slot):
            return acc[:, slot, :, 0:TH]

        def flat(t):
            return t[:].rearrange("p a n -> p (a n)")

        def halves(ap):
            return ap.rearrange("p (a n) -> p a n", a=2)

        def m_halves(b):
            return m4[:, b:b + 2, 0:TH]

        def column(t, j):
            if isinstance(j, int):
                return t[:, j]
            return t[:, bass.ds(j, 1)].rearrange("p a n -> p (a n)")

        sems = []

        def sem(name):
            s = ctx.enter_context(nc.semaphore(name))
            sems.append(s)
            return s
        y_out = sem("y_out")
        cst_in = sem("cst_in")
        sems.clear()
        x_part = [sem(f"x_part{i}") for i in range(KD // 2)]
        raw_in = [sem("raw_in0"), sem("raw_in1")]
        signals = {
            "hi_done": "a weight tile's rounded part is in the ring (ScalarE)",
            "lo_done": "... and its rest (VectorE)",
            "acc_done": "an output chunk is accumulated (TensorE)",
            "acc_out": "... and taken out of PSUM (VectorE)",
            "par_in": "the layer's parameters",
            "gm_in": "the next layer's gain",
            "x_in": "x is back from DRAM",
            "kts_in": "k cache",
            "vs_in": "v cache",
            "vnew_in": "the decode tokens' new v rows",
            "conv_in": "both convolutions' states",
            "s0_in": "GLA states of heads 0, 1",
            "s1_in": "... of heads 2, 3",
            "kv_out": "new k and v caches",
            "sc_out": "short convolution's states",
            "cf_out": "wide convolution's states",
            "s0_out": "decode tokens' GLA states",
            "sh_out": "the prompt's GLA state",
            "xhi_done": "x * gain, rounded",
            "xlo_done": "... and its rest",
            "ss_sq": "a k tile of x squared",
            "ss_done": "... added to ssum",
            "ss_mm": "sum of x squared over the channels, in banks 0 and 1",
            "rstd_ln": "its logarithm",
            "rstd_done": "rstd",
            "e_done": "a sigmoid",
            "o_hi": "a branch output's chunk, rounded",
            "o_split": "... and its rest",
            "add_done": "a gated chunk is added to merged (GpSimd)",
            "mg_done": "merged's chunk is complete",
            "m_hi": "... rounded",
            "m_split": "... and its rest",
            "cf_written": "the wide convolution's input chunk",
            "sc_written": "the short convolution's input chunk",
            "sc_o": "branch A's chunk",
            "conv_done": "VectorE's chunks of the wide convolution",
            "qk_sq": "squares",
            "qk_ss": "sums over a head, in banks 0 and 1",
            "qk_ln": "their logarithm: the banks are read",
            "qk_rn": "the factor",
            "qk_n": "normalised chunk",
            "qk_r": "its rotated half, in banks 2 and 3",
            "qk_rot": "... times the sine: the banks are read",
            "qk_out": "rotated chunk",
            "v_t": "v transposed, in banks 0 and 1",
            "v_copied": "... in SBUF",
            "qz_zero": "the block-diagonal q is cleared",
            "s_q": "... and filled",
            "s_scores": "scores, in bank 0",
            "s_sub": "their negated maximum",
            "s_exp": "exponentials",
            "s_p": "probabilities",
            "s_t": "... transposed, in bank 2",
            "s_tc": "... in SBUF",
            "s_pv": "values, in bank 3",
            "s_out": "... in q's place",
            "a_s": "scores, in banks 0 and 1",
            "a_max": "masked scores in SBUF, and their negated maximum",
            "a_exp": "exponentials",
            "a_p": "probabilities",
            "a_t": "... transposed, in banks 2 and 3",
            "a_tc": "... in SBUF",
            "a_o": "values, in bank 2",
            "a_out": "... in q's place",
            "gv_t": "v transposed, in all banks",
            "gv_c": "... in SBUF",
            "g_z": "the decay's low-rank product, in all banks",
            "g_abs": "-|z|",
            "g_log": "ln(1 + exp(-|z|))",
            "g_scan": "log decay summed within the chunks",
            "g_e1": "its exponential",
            "g_e2": "... and inverse",
            "g_gap": "log decay from a token to its chunk's end",
            "g_e3": "its exponential",
            "g_prep": "q and k with their decays",
            "g_kdt": "decayed k and the decode tokens' k, v transposed, in all banks",
            "g_kdc": "... in SBUF",
            "g_u": "each chunk's k v^T, in all banks",
            "g_state": "the state after each chunk",
            "gg_done": "silu of the output gate",
            "ga_a": "scores, in banks 0 and 1",
            "ga_m": "... masked, in SBUF",
            "ga_o": "output, in banks 2 and 3",
            "ga_out": "... in gv's place",
            "gqz_zero": "the block-diagonal q is cleared",
            "gqz_done": "... and filled",
            "gs_v": "block-diagonal v",
            "gs_mm": "k v^T, in banks 0 and 1",
            "gs_s": "new states",
            "gs_q": "q times the states, in bank 2",
            "gs_o": "... in SBUF",
            "gs_t": "... transposed, in bank 3",
            "gs_g": "... in gv's place",
            "gn_sq": "squares",
            "gn_mm": "their sum over a head",
            "gn_r": "rstd",
            "gn_o": "gated output",
            "ln_add": "the sum over the four chunks",
            "ln_sum": "the sum over the channels, in banks 0 and 1",
            "ln_xc": "centred",
            "ln_sq": "squared",
            "ln_var": "their sum over the channels, in banks 0 and 1",
            "ln_r": "rstd",
            "ln_y": "normalised chunk",
            "ln_e": "its sigmoid",
            "ln_o": "silu: branch B's chunk",
            "h_x": "exp(-gate)",
            "h_r": "ln(1 + exp(-gate))",
            "h_e": "sigmoid(gate)",
            "h_t": "silu(gate)",
            "h_h": "silu(gate) * up",
            "h_hi": "... rounded",
            "h_lo": "... and its rest",
            "vec_order": "VectorE",
            "act_order": "ScalarE",
            "pool_order": "GpSimd",
        }
        s = {n: sem(n) for n in signals}
        last_sem, first_sem = sems[-1], sems[0]

        class Steps:

            def __init__(self, eng, order):
                self.eng, self.order, self.count = eng, order, {}

            def __call__(self, ins, name=None):
                name = name or self.order
                self.count[name] = self.count.get(name, 0) + 1
                ins.then_inc(s[name], 1)
                self.last = name, self.count[name]
                return self.last

            def settled(self):
                self.need(self.last)

            def need(self, *points):
                for name, value in points:
                    self.eng.wait_ge(s[name], value)

        with nc.Block() as block:
            @block.sync
            def _(sp):
                for k in range(0, KD, 2):
                    sp.dma_start(x[:, k:k + 2], xt[:, k:k + 2]).then_inc(x_part[k // 2], 16)
                sp.dma_start(raw[:, 0], wt[0]).then_inc(raw_in[0], 16)
                sp.dma_start(raw[:, 1], wt[1]).then_inc(raw_in[1], 16)
                sp.dma_start(cs[:], cst).then_inc(cst_in, 16)
                sp.dma_start(glam[:], glam_d).then_inc(cst_in, 16)
                sp.dma_start(scanm[:], scan_d).then_inc(cst_in, 16)
                sp.dma_start(yt, xt).then_inc(y_out, 16)
                sp.wait_ge(raw_in[1], 16)

            @block.scalar
            def _(a):
                a.dma_start(gmix[:], gm[0]).then_inc(s["gm_in"], 16)
                a.preload_act_table_set("natural_log_exp_and_others")
                a.wait_ge(s["gm_in"], 16)
                for k in range(KD):
                    if k % 2 == 0:
                        a.wait_ge(x_part[k // 2], 16)
                    nc.scalar.activation(xhi[:, k], x[:, k], ACT.Copy, scale=gmix[:, k:k + 1])\
                        .then_inc(s["xhi_done"], 1)
                    if k >= 2:
                        a.wait_ge(s["ss_done"], k - 1)
                    nc.scalar.activation(tmp[:, k % 2], x[:, k], ACT.Square).then_inc(s["ss_sq"], 1)
                a.wait_ge(raw_in[0], 16)
                for t in range(2):
                    nc.scalar.activation(whi[:, t], raw[:, 0, t * 1024:t * 1024 + 1024], ACT.Copy)\
                        .then_inc(s["hi_done"], 1)

            @block.vector
            def _(dve):
                nc.vector.memset(small[:], 0.0)
                dve.wait_ge(s["gm_in"], 16)
                for k in range(KD):
                    dve.wait_ge(s["xhi_done"], k + 1)
                    nc.vector.scalar_tensor_tensor(out=xlo[:, k], in0=x[:, k], scalar=gmix[:, k:k + 1],
                                                   in1=xhi[:, k].bitcast(F32), op0=ALU.mult, op1=ALU.subtract)
                    dve.wait_ge(s["ss_sq"], k + 1)
                    if k == 0:
                        nc.vector.tensor_copy(ssum[:], tmp[:, 0]).then_inc(s["ss_done"], 1)
                    else:
                        dve.wait_ge(s["ss_done"], k)
                        nc.vector.tensor_tensor(ssum[:], ssum[:], tmp[:, k % 2], ALU.add).then_inc(s["ss_done"], 1)
                for t in range(2):
                    dve.wait_ge(s["hi_done"], t + 1)
                    nc.vector.tensor_tensor(wlo[:, t], raw[:, 0, t * 1024:t * 1024 + 1024],
                                            whi[:, t].bitcast(F32), ALU.subtract)
        nc.all_engine_barrier(sems_to_clear=range(first_sem.num, last_sem.num + 1))

        with nc.Fori(0, DEPTH) as layer:
            with nc.Block() as block:

                @block.sync
                def _(sp):
                    def unit(u, e, width):
                        if not (isinstance(u, int) and u == 2):
                            sp.wait_ge(s["lo_done"], u * 2 - 4)
                        sp.dma_start(raw[:, e, 0:width], wt[bass.ds(layer * UNITS + u, 1), :, 0:width]
                                     .rearrange("a p n -> (a p) n")).then_inc(raw_in[e], 16)

                    def units(first, last, width):
                        with sp.Fori(0, (last - first) // 2) as i:
                            for e in range(2):
                                unit(i * 2 + (first + e), e, width)
                    for e in range(2):
                        unit(2 + e, e, 2048)
                    units(4, T_F2A // 2, 2048)
                    units(T_F2A // 2, T_F1B // 2, FA * P)
                    units(T_F1B // 2, T_F2B // 2, 2048)
                    units(T_F2B // 2, UNITS, FB * P)
                    for e in range(2):
                        unit(UNITS + e, e, 2048)
                    sp.wait_ge(raw_in[1], 16 * (UNITS // 2))

                @block.tensor
                def _(pe):
                    def product(out, a_hi, a_lo, b_hi, b_lo, first, last):
                        for n, (a, b) in enumerate(((a_lo, b_hi), (a_hi, b_lo), (a_hi, b_hi))):
                            for h in range(2):
                                ins = nc.tensor.matmul(out[:, h], a, b[:, h * TH:h * TH + TH],
                                                       start=first and n == 0, stop=last and n == 2)
                        return ins

                    def tile_ready(t):
                        if not (isinstance(t, int) and t < 2):
                            pe.wait_ge(s["lo_done"], t - 1)

                    def sum_over_channels(bank, operands, name):
                        n = len(operands)
                        for k, o in enumerate(operands):
                            for h in range(2):
                                ins = nc.tensor.matmul(m4[:, bank + h, 0:TH], ones, o[:, h * TH:h * TH + TH],
                                                       start=k == 0, stop=k == n - 1)
                        ins.then_inc(s[name], 1)

                    def side(n):
                        if n == 0:
                            pe.wait_ge(cst_in, 48)
                            sum_over_channels(0, [ssum], "ss_mm")
                        c = n - (S_AQ + 1)
                        if 0 <= c < 5:
                            pe.wait_ge(s["qk_sq"], c + 1)
                            if c == 0:
                                pe.wait_ge(s["rstd_done"], 1)
                            if c >= 1:
                                pe.wait_ge(s["qk_ln"], c)
                            for h in range(2):
                                ins = nc.tensor.matmul(m4[:, h, 0:TH], cst_("ones64"), gt[:, 0, h * TH:h * TH + TH],
                                                       start=True, stop=True)
                            ins.then_inc(s["qk_ss"], 1)
                        c = n - (S_AQ + 3)
                        if 0 <= c < 5:
                            pe.wait_ge(s["qk_n"], c + 1)
                            if c >= 1:
                                pe.wait_ge(s["qk_rot"], c)
                            src = q[:, c] if c < GROUP else kt[:]
                            for h in range(2):
                                ins = nc.tensor.matmul(m4[:, 2 + h, 0:TH], cst_("rot"), src[:, h * TH:h * TH + TH],
                                                       start=True, stop=True)
                            ins.then_inc(s["qk_r"], 1)
                        if n == S_AV + 3:
                            pe.wait_ge(s["acc_out"], S_AV + 1)
                            pe.wait_ge(s["qk_ln"], 5)
                            for b in range(NBLK):
                                nc.tensor.transpose(m4[:, 0, b * P:b * P + P], vt[:, b * P:b * P + P], ident)
                            nc.tensor.transpose(m4[0:NS, 1, 0:P], vt[:, SEQ:T], ident).then_inc(s["v_t"], 1)
                        if n == SATT:
                            pe.wait_ge(s["s_q"], 1)
                            pe.wait_ge(s["v_copied"], 1)
                            for b in range(NS):
                                ins = nc.tensor.matmul(m4[0:NQ, 0, 0:P], flat(qz)[:, b * NQ:b * NQ + NQ], kts[:, b],
                                                       start=b == 0, stop=b == NS - 1)
                            ins.then_inc(s["s_scores"], 1)
                        if n == SATT + 2:
                            pe.wait_ge(s["s_p"], 1)
                            pe.wait_ge(s["qk_rot"], 5)
                            nc.tensor.transpose(m4[:, 2, 0:NQ], sprob[:], cst_("ident", NQ)[:, 0:NQ])\
                                .then_inc(s["s_t"], 1)
                        if n == SATT + 3:
                            pe.wait_ge(s["s_tc"], 1)
                            pe.wait_ge(s["vnew_in"], 16 * NS)
                            pe.wait_ge(s["vs_in"], 16)
                            for b in range(NS):
                                ins = nc.tensor.matmul(m4[:, 3, b * NS:b * NS + NS], vs[:, b], pts[:, b],
                                                       start=True, stop=True)
                            ins.then_inc(s["s_pv"], 1)
                        for g in range(NBLK * NKV):
                            blk, kv = g // NKV, g % NKV
                            rows = slice(kv * HEAD, kv * HEAD + HEAD)
                            k0 = 0 if blk else 1
                            if n == ATT[g] + 3:
                                pe.wait_ge(s["a_tc"], g + 1)
                                for kc in range(k0, 2):
                                    ins = nc.tensor.matmul(m4[rows, 2], vb[:, blk - 1 + kc, rows], probt[:, kc],
                                                           start=kc == k0, stop=kc == 1)
                                ins.then_inc(s["a_o"], 1)
                        for g in range(NBLK * NKV):
                            blk, kv = g // NKV, g % NKV
                            rows = slice(kv * HEAD, kv * HEAD + HEAD)
                            k0 = 0 if blk else 1
                            if n == ATT[g]:
                                if g:
                                    pe.wait_ge(s["a_max"], g)
                                for h in range(GROUP):
                                    ins = nc.tensor.matmul(
                                        m4[:, h // 2, (h % 2) * 256 + k0 * P:(h % 2) * 256 + 256],
                                        q[rows, h, blk * P:blk * P + P],
                                        kt[rows, (blk - 1 + k0) * P:(blk + 1) * P], start=True, stop=True)
                                ins.then_inc(s["a_s"], 1)
                            if n == ATT[g] + 2:
                                pe.wait_ge(s["a_p"], g + 1)
                                if g:
                                    pe.wait_ge(s["a_out"], g)
                                else:
                                    pe.wait_ge(s["s_out"], 2)
                                for kc in range(k0, 2):
                                    for h in range(GROUP):
                                        ins = nc.tensor.transpose(m4[:, 2 + kc, h * P:h * P + P],
                                                                  prob[:, h, kc * P:kc * P + P], ident)
                                ins.then_inc(s["a_t"], 1)
                        if n == G_VT:
                            pe.wait_ge(s["a_out"], 8)
                            for b in range(NBLK):
                                for h in range(4):
                                    ins = nc.tensor.transpose(m4[:, b, h * P:h * P + P], gv[:, h, b * P:b * P + P],
                                                              ident)
                            ins.then_inc(s["gv_t"], 1)
                        if n == G_Z:
                            pe.wait_ge(s["gv_c"], 1)
                            for p in range(2):
                                for h in range(2):
                                    ins = nc.tensor.matmul(m4[:, 2 * p + h, 0:TH], par_("wg", p * P, P, 16),
                                                           tmp[0:16, 2, h * TH:h * TH + TH], start=True, stop=True)
                            ins.then_inc(s["g_z"], 1)
                        if n == G_KDT:
                            pe.wait_ge(s["g_prep"], 2)
                            pe.wait_ge(s["ln_xc"], 1)
                            for b in range(NBLK):
                                for p in range(2):
                                    o = (b % 2) * 256 + p * P
                                    nc.tensor.transpose(m4[:, b // 2, o:o + P], gb[:, p, b * P:b * P + P], ident)
                            for p in range(2):
                                nc.tensor.transpose(m4[0:NS, 2, p * P:p * P + P], gb[:, p, SEQ:T], ident)
                            for h in range(4):
                                ins = nc.tensor.transpose(m4[0:NS, 3, h * P:h * P + P], gv[:, h, SEQ:T], ident)
                            ins.then_inc(s["g_kdt"], 1)
                        if n == G_U:
                            pe.wait_ge(s["g_kdc"], 1)
                            pe.wait_ge(s["ln_r"], 1)
                            for c in range(NCHUNK):
                                r = slice((c % 2) * CHUNK, (c % 2) * CHUNK + CHUNK)
                                for h in range(4):
                                    o = ((c // 2) % 2) * 256 + (h // 2) * P
                                    ins = nc.tensor.matmul(
                                        m4[(h % 2) * HEAD:(h % 2) * HEAD + HEAD, (c % 2) * 2 + c // 4, o:o + P],
                                        kdt[r, c // 2, h * HEAD:h * HEAD + HEAD], vtok[r, c // 2, h * P:h * P + P],
                                        start=True, stop=True)
                            ins.then_inc(s["g_u"], 1)
                        if n == LN_SUM:
                            pe.wait_ge(s["g_abs"], 1)
                            pe.wait_ge(s["ln_add"], 1)
                            sum_over_channels(0, [ssum], "ln_sum")
                        if n == LN_VAR:
                            pe.wait_ge(s["g_kdc"], 1)
                            pe.wait_ge(s["ln_add"], 2)
                            sum_over_channels(0, [ssum], "ln_var")
                        for b in range(NBLK):
                            if n == G_A[b] + 1:
                                pe.wait_ge(s["ga_m"], b + 1)
                                if b:
                                    pe.wait_ge(s["ga_out"], b)
                                for h in range(4):
                                    p, hh = h // 2, h % 2
                                    r = slice(hh * HEAD, hh * HEAD + HEAD)
                                    nc.tensor.matmul(m4[:, 2 + hh, p * P:p * P + P], vtok[:, b, h * P:h * P + P],
                                                     am[:, 2 * hh + p], start=True, stop=False)
                                    for cc in range(2):
                                        ch = 2 * b + cc
                                        if ch == 0:
                                            continue
                                        t0 = ch * CHUNK
                                        o = p * P + cc * CHUNK
                                        ins = nc.tensor.matmul(m4[:, 2 + hh, o:o + CHUNK], sh[r, ch - 1, p],
                                                               gq[r, p, t0:t0 + CHUNK], start=False, stop=cc == 1)
                                ins.then_inc(s["ga_o"], 1)
                        for b in range(NBLK):
                            if n == G_A[b]:
                                if b == 0:
                                    pe.wait_ge(s["g_state"], 1)
                                else:
                                    pe.wait_ge(s["ga_m"], b)
                                for p in range(2):
                                    for hh in range(2):
                                        r = slice(hh * HEAD, hh * HEAD + HEAD)
                                        ins = nc.tensor.matmul(m4[:, hh, p * P:p * P + P], gk[r, p, b * P:b * P + P],
                                                               gq[r, p, b * P:b * P + P], start=True, stop=True)
                                ins.then_inc(s["ga_a"], 1)
                        for p in range(2):
                            if n == G_S[p]:
                                pe.wait_ge(s["gs_v"], p + 1)
                                pe.wait_ge(s[f"s{p}_in"], 16)
                                if p == 0:
                                    pe.wait_ge(s["ga_out"], NBLK)
                                else:
                                    pe.wait_ge(s["gs_s"], 1)
                                for hh in range(2):
                                    h = 2 * p + hh
                                    for half in range(2):
                                        ins = nc.tensor.matmul(
                                            m4[hh * HEAD:hh * HEAD + HEAD, half], kds[:, h * HEAD:h * HEAD + HEAD],
                                            vbd[hh][:, 4 * half:4 * half + 4].rearrange("k b n -> k (b n)"),
                                            start=True, stop=True)
                                ins.then_inc(s["gs_mm"], 1)
                            if n == G_S[p] + 1:
                                pe.wait_ge(s["gs_s"], p + 1)
                                pe.wait_ge(s["gqz_done"], 1)
                                for b in range(NS):
                                    ins = nc.tensor.matmul(
                                        m4[0:2 * NS, 2, 0:P],
                                        gqz[:, p].rearrange("p a n -> p (a n)")[:, b * 2 * NS:b * 2 * NS + 2 * NS],
                                        s0[p][:, b], start=b == 0, stop=b == NS - 1)
                                ins.then_inc(s["gs_q"], 1)
                            if n == G_S[p] + 2:
                                pe.wait_ge(s["gs_o"], p + 1)
                                if p:
                                    pe.wait_ge(s["gs_g"], 1)
                                nc.tensor.transpose(m4[:, 3, 0:2 * NS], o16, cst_("ident", 2 * NS)[:, 0:2 * NS])\
                                    .then_inc(s["gs_t"], 1)
                        h = n - G_N
                        if 0 <= h < 4:
                            pe.wait_ge(s["gn_sq"], h + 1)
                            if h == 0:
                                pe.wait_ge(s["gs_s"], 2)
                            if h == 1:
                                pe.wait_ge(s["gs_g"], 2)
                            if h >= 2:
                                pe.wait_ge(s["gn_r"], h - 1)
                            sum_over_channels(2 * (h % 2), [tmp[:, 2]], "gn_mm")

                    done = 0
                    order = {0: 0, 2: 1, 1: 2, 3: 3}
                    for n, (kind, c) in enumerate(SLOTS):
                        if n >= 2:
                            pe.wait_ge(s["acc_out"], n - 1)
                        tiles, off = TILE_OF[n]
                        tile_ready(tiles[-1])
                        if isinstance(kind, tuple) and kind[0] == "branch":
                            i, buf = order[kind[1]], kind[1] in (1, 2)
                            for k in range(KB):
                                if c == 0:
                                    pe.wait_ge(s["o_split"], 4 * i + k + 1)
                                w = slice(off + k * P, off + k * P + P)
                                ins = product(acc_of(n % 2), whi[:, tiles[0] % 4, w], wlo[:, tiles[0] % 4, w],
                                              ohi[buf][:, k], olo[buf][:, k], k == 0, k == KB - 1)
                        else:
                            per = KD // len(tiles)
                            for k in range(KD):
                                t = tiles[k // per] % 4
                                w = slice((k % per) * P, (k % per) * P + P)
                                ins = product(acc_of(n % 2), whi[:, t, w], wlo[:, t, w], xhi[:, k], xlo[:, k],
                                              k == 0, k == KD - 1)
                        ins.then_inc(s["acc_done"], 1)
                        side(n)

                    def whole(n, t, e, bh, bl, ready=None, first=0):
                        pe.wait_ge(s["acc_out"], n - 1)
                        tile_ready(t)
                        ts = (e + first) % 4
                        for k in range(KD):
                            if ready is not None:
                                pe.wait_ge(s[ready], k + 1)
                            w = slice(k * P, k * P + P)
                            ins = product(acc_of(e % 2), whi[:, ts, w], wlo[:, ts, w], bh[:, k], bl[:, k],
                                          k == 0, k == KD - 1)
                        ins.then_inc(s["acc_done"], 1)

                    pe.wait_ge(s["acc_out"], N_O)
                    for e in range(2):
                        tile_ready(T_O + e)
                    for ks in (range(KD - 1), range(KD - 1, KD)):
                        for e in range(2):
                            for k in ks:
                                pe.wait_ge(s["m_split"], k + 1)
                                w = slice(k * P, k * P + P)
                                ins = product(acc_of(e), whi[:, (T_O + e) % 4, w], wlo[:, (T_O + e) % 4, w],
                                              mhi[:, k], mlo[:, k], k == 0, k == KD - 1)
                            if ks[-1] == KD - 1:
                                ins.then_inc(s["acc_done"], 1)
                    for e in range(2, 4):
                        whole(N_O + e, T_O + e, e, mhi, mlo, None, T_O)
                    with pe.Fori(1, KD // 4) as i:
                        for e in range(4):
                            whole(i * 4 + (N_O + e), i * 4 + (T_O + e), e, mhi, mlo, None, T_O)

                    def ffn_in(n0, t0, count, first_half):
                        whole(n0, t0, 0, xhi, xlo, "xlo_done" if first_half else None, t0)
                        if first_half:
                            pe.wait_ge(s["ss_done"], KD)
                            sum_over_channels(0, [ssum], "ss_mm")
                        for e in range(1, 4):
                            whole(n0 + e, t0 + e, e, xhi, xlo, None, t0)
                        with pe.Fori(1, count // 2) as i:
                            for e in range(4):
                                whole(i * 4 + (n0 + e), i * 4 + (t0 + e), e, xhi, xlo, None, t0)

                    def ffn_out(n0, t0, count, before):
                        half = count // 2

                        def chunk(n, t, e, ready):
                            pe.wait_ge(s["acc_out"], n - 1)
                            tile_ready(t + 1)
                            for k in range(count):
                                if ready:
                                    pe.wait_ge(s["h_lo"], before + k + 1)
                                ts = (2 * e + k // half + t0) % 4
                                w = slice((k % half) * P, (k % half) * P + P)
                                ins = product(acc_of(e), whi[:, ts, w], wlo[:, ts, w], hhi[:, k], hlo[:, k],
                                              k == 0, k == count - 1)
                            ins.then_inc(s["acc_done"], 1)
                        for e in range(2):
                            chunk(n0 + e, t0 + 2 * e, e, e == 0)
                        with pe.Fori(1, KD // 2) as i:
                            for e in range(2):
                                chunk(i * 2 + (n0 + e), i * 4 + (t0 + 2 * e), e, False)
                    ffn_in(N_F1A, T_F1A, FA, True)
                    ffn_out(N_F2A, T_F2A, FA, 0)
                    ffn_in(N_F1B, T_F1B, FB, False)
                    ffn_out(N_F2B, T_F2B, FB, FA)

                @block.scalar
                def _(a):
                    st = Steps(a, "act_order")

                    def act(out, in_, func=ACT.Copy, name=None, **kw):
                        return st(nc.scalar.activation(out, in_, func, **kw), name)

                    def load(out, in_, name):
                        a.dma_start(out, in_).then_inc(s[name], 16)

                    def of(d):
                        n = len(d.shape)
                        v = d[bass.ds(layer, 1)]
                        names = " ".join("abcdef"[:n - 1])
                        return v.rearrange(f"z {names} -> (z a) {' '.join('bcdef'[:n - 2])}")

                    def hi(e, ts, length, count=None, free=None, off=0):
                        if count is not None:
                            a.wait_ge(raw_in[e], count)
                        if free is not None:
                            a.wait_ge(s["acc_done"], free)
                        nc.scalar.activation(whi[:, ts, 0:length], raw[:, e, off:off + length], ACT.Copy)\
                            .then_inc(s["hi_done"], 1)

                    def mix_hi(t):
                        hi((t // 2) % 2, t % 4, TILE_LEN[t], 16 * (t // 4) if t % 2 == 0 and t >= 4 else None,
                           LAST_USE[t - 4] + 1 if t >= 4 else None, (t % 2) * 1024)

                    def rsqrt(out, in_, scale, eps, first, last):
                        st.need(act(out, in_, ACT.Ln, first, scale=scale, bias=eps))
                        act(out.rearrange("p a n -> p (a n)"), out.rearrange("p a n -> p (a n)"), ACT.Exp, last,
                            scale=-0.5)

                    def sigmoid(out, in_, name):
                        st.need(act(out, in_, ACT.Exp, scale=-1.0))
                        st.need(act(out, out, ACT.Ln, bias=1.0))
                        act(out, out, ACT.Exp, name, scale=-1.0)

                    hi_next = [2]
                    for t in range(2, 4):
                        mix_hi(t)
                        hi_next[0] += 1
                    load(pr[:], of(par), "par_in")
                    load(kts[:, :, 0:WIN - 1], of(kc), "kts_in")
                    load(cfs[:, :, :, 0:W2 - 1], of(ccst), "conv_in")
                    load(scs[:, :, :, 0:W1 - 1], of(scst), "conv_in")
                    load(gmix[:], gm[bass.ds(layer + 1, 1)].rearrange("z p k -> (z p) k"), "gm_in")

                    def side(n):
                        if n == 2:
                            a.wait_ge(s["par_in"], 16)
                            a.wait_ge(y_out, layer * (KD * 16) + 16)
                            load(vs[0:WIN - 1], of(vc), "vs_in")
                        if n == 8:
                            a.wait_ge(s["cf_written"], KB)
                            load(of(o_cc), cfu[:, :, SEQ:SEQ + W2 - 1], "cf_out")
                            load(of(o_ccs), cfs[:, :, :, 1:W2], "cf_out")
                        if n == S_GATE_A:
                            a.wait_ge(s["sc_written"], KB)
                            load(of(o_sc), scu[:, :, SEQ:SEQ + W1 - 1], "sc_out")
                            load(of(o_scs), scs[:, :, :, 1:W1], "sc_out")
                        c = n - (S_AQ + 2)
                        if 0 <= c < 5:
                            a.wait_ge(s["qk_ss"], c + 1)
                            if c:
                                a.wait_ge(s["qk_n"], c)
                            rsqrt(halves(gt[:, 1]), m_halves(0), 1.0 / HEAD, RMS_EPS, "qk_ln", "qk_rn")
                        if n == SATT:
                            a.wait_ge(s["v_t"], 1)
                            act(vb[:].rearrange("p b n -> p (b n)"), m4[:, 0], name="act_order")
                            st.need(act(vnew, m4[0:NS, 1, 0:P], name="v_copied"))
                            a.wait_ge(s["vs_in"], 16)
                            for b in range(NS):
                                load(vs[WIN - 1:WIN, b], vnew[b:b + 1], "vnew_in")
                        if n == SATT + 1:
                            a.wait_ge(s["s_sub"], 1)
                            act(sprob[:], sprob[:], ACT.Exp, bias=snmax, accum_out=slsum)
                            act(sesink, par_("sink64", rows=NQ), ACT.Exp, "s_exp", bias=snmax)
                            a.wait_ge(s["qk_out"], 5)
                            a.wait_ge(s["s_q"], 1)
                            a.wait_ge(s["vnew_in"], 16 * NS)
                            load(of(o_k), kt[:, SEQ - WIN:SEQ], "kv_out")
                            load(of(o_v), vt[:, SEQ - WIN:SEQ], "kv_out")
                            load(of(o_ks), kts[:], "kv_out")
                            load(of(o_vs), vs[:], "kv_out")
                        for g in range(NBLK * NKV):
                            blk, kv = g // NKV, g % NKV
                            rows = slice(kv * HEAD, kv * HEAD + HEAD)
                            k0 = 0 if blk else 1
                            if n == ATT[g] + 3:
                                a.wait_ge(s["a_t"], g + 1)
                                for kc_ in range(k0, 2):
                                    act(probt[:, kc_], m4[:, 2 + kc_], name="a_tc" if kc_ == 1 else None)
                            if n == ATT[g] + 4:
                                a.wait_ge(s["a_o"], g + 1)
                                act(q[rows, :, blk * P:blk * P + P],
                                    m4[rows, 2].rearrange("p (h n) -> p h n", h=GROUP), name="a_out")
                            if n == ATT[g] + 1:
                                a.wait_ge(s["a_max"], g + 1)
                                for h in range(GROUP):
                                    act(prob[:, h, k0 * P:2 * P], prob[:, h, k0 * P:2 * P], ACT.Exp,
                                        bias=nmax[:, h:h + 1], accum_out=lsum[:, h:h + 1])
                                act(esink, esink, ACT.Exp, "a_exp")
                        c = n - (ATT[-1] + 5)
                        if 0 <= c < KB:
                            if c == 0:
                                st.need(("a_out", 8))
                                a.wait_ge(s["s_out"], 2)
                                a.wait_ge(s["kv_out"], 64)
                                load(s0[0][:], gst_of(0), "s0_in")
                            act(ohi[1][:, c], q[:, c], name="o_hi")
                        if n == G_VT + 1:
                            a.wait_ge(s["gv_t"], 1)
                            for b in range(NBLK):
                                act(vtok[:, b], m4[:, b], name="gv_c" if b == NBLK - 1 else None)
                        for p in range(2):
                            if n == G_Z + 1 + 2 * p:
                                za, ze = gla_tmp(p)
                                a.wait_ge(s["g_abs"], p + 1)
                                st.need(act(ze, ze, ACT.Exp))
                                act(ze, ze, ACT.Ln, "g_log", bias=1.0)
                                a.wait_ge(s["g_scan"], p + 1)
                                act(ze, gb[:, p], ACT.Exp, "g_e1", scale=1.0 / 16)
                                act(za, gb[:, p], ACT.Exp, "g_e2", scale=-1.0 / 16)
                            if n == G_Z + 2 + 2 * p:
                                za, ze = gla_tmp(p)
                                a.wait_ge(s["g_gap"], p + 1)
                                act(ze[:, 0:SEQ], ze[:, 0:SEQ], ACT.Exp, "g_e3", scale=1.0 / 16)
                        if n == G_KDT + 1:
                            a.wait_ge(s["g_kdt"], 1)
                            act(kdt[:].rearrange("p (c b) n -> p c (b n)", c=2), m4[:, 0:2])
                            act(kds, m4[0:NS, 2, 0:2 * P])
                            act(vst[:], m4[0:NS, 3], name="g_kdc")
                        if n == G_U + 2:
                            a.wait_ge(s["g_state"], 1)
                            load(o_g_of(), sh[:, NCHUNK - 1], "sh_out")
                        if n == LN_XC:
                            a.wait_ge(s["ln_xc"], 1)
                            a.wait_ge(s["cf_out"], 32)
                            for c in range(KB):
                                act(cfu[:, c, 0:T], cacc[:, c], ACT.Square, "ln_sq" if c == KB - 1 else None)
                        if n == LN_VAR + 1:
                            a.wait_ge(s["ln_var"], 1)
                            rsqrt(halves(tmp[:, 0]), m_halves(0), 1.0 / BW, LN_EPS, None, "ln_r")
                        c = n - (LN_Y + 1)
                        if 0 <= c < KB:
                            a.wait_ge(s["ln_y"], c + 1)
                            sigmoid(cfu[:, c, 0:T], cacc[:, c], "ln_e")
                        for b in range(NBLK):
                            if n == G_A[b] + 2:
                                a.wait_ge(s["ga_o"], b + 1)
                                for hh in range(2):
                                    act(gv[:, hh:4:2, b * P:b * P + P],
                                        m4[:, 2 + hh, 0:256].rearrange("p (h n) -> p h n", h=2),
                                        name="ga_out" if hh else None)
                        c = n - S_GATE_B
                        if 0 <= c < KB:
                            if c == 0:
                                a.wait_ge(s["acc_done"], S_GATE_B)
                            a.wait_ge(s["ln_o"], c + 1)
                            act(ohi[1][:, c], cacc[:, c], name="o_hi")
                        if n == LN_Y + KB + 2:
                            a.wait_ge(s["ln_o"], KB)
                            load(s0[1][:], gst_of(1), "s1_in")
                        for p in range(2):
                            if n == G_S[p] + 2:
                                a.wait_ge(s["gs_q"], p + 1)
                                if p:
                                    a.wait_ge(s["gs_t"], 1)
                                else:
                                    a.wait_ge(s["o_split"], 1)
                                act(o16, m4[0:2 * NS, 2, 0:P], name="gs_o")
                                load(gs_out_of(p), s0[p][:], "s0_out")
                        h = n - (G_N + 1)
                        if 0 <= h < 4:
                            a.wait_ge(s["gn_mm"], h + 1)
                            if h:
                                a.wait_ge(s["gn_o"], h)
                            else:
                                a.wait_ge(s["gs_s"], 2)
                            b = 2 * (h % 2)
                            rsqrt(halves(ge[:]), m_halves(b), 1.0 / P, RMS_EPS, None, "gn_r")
                        h = n - G_N
                        if 0 <= h < 4:
                            if h:
                                a.wait_ge(s["gn_mm"], h)
                            else:
                                a.wait_ge(s["gs_mm"], 2)
                            a.wait_ge(s["gs_g"], h // 2 + 1)
                            act(tmp[:, 2], gv[:, h], ACT.Square, "gn_sq")
                        h = n - (G_N + 2)
                        if 0 <= h < 4:
                            a.wait_ge(s["gn_o"], h + 1)
                            act(ohi[0][:, h], gv[:, h], name="o_hi")
                        if n == G_N + 6:
                            a.wait_ge(s["o_split"], 16)
                            load(x[:], yt, "x_in")

                    def o_g_of():
                        return o_g[bass.ds(layer, 1)].rearrange("z p c n -> (z p) c n")

                    def gst_of(p):
                        return gst[bass.ds(layer, 1), p].rearrange("z p b n -> (z p) b n")

                    def gs_out_of(p):
                        return o_gs[bass.ds(layer, 1), p].rearrange("z p b n -> (z p) b n")

                    def gla_tmp(p):
                        return (tmp[:, 2], ge[:]) if p == 0 else (tmp[:, 0], tmp[:, 1])

                    for n, (kind, c) in enumerate(SLOTS):
                        side(n)
                        while hi_next[0] <= last_tile(n + 3):
                            mix_hi(hi_next[0])
                            hi_next[0] += 1
                        if n == 0:
                            a.wait_ge(s["ss_mm"], 1)
                            rsqrt(halves(rstd[:]), m_halves(0), 1.0 / D_MODEL, RMS_EPS, "rstd_ln", "rstd_done")
                        gate = isinstance(kind, tuple) and kind[0] == "gate"
                        if kind == "cfb" or gate or kind == "gg":
                            a.wait_ge(s["acc_out"], n + 1)
                            dst = tmp[:, c % 2] if kind == "gg" else gt[:, c % 4 if gate else c % 2]
                            sigmoid(dst, gg[:, c] if kind == "gg" else dst, "e_done")
                        if kind in ("aq", "ak"):
                            i = n - S_AQ
                            a.wait_ge(s["acc_out"], n + 1)
                            if i:
                                a.wait_ge(s["qk_ss"], i)
                            act(gt[:, 0], q[:, c] if kind == "aq" else kt[:], ACT.Square, "qk_sq")
                        if kind == "scb":
                            a.wait_ge(s["sc_o"], c + 1)
                            act(ohi[0][:, c], sct[:, c % 2], name="o_hi")
                        if kind == ("branch", 3):
                            a.wait_ge(s["mg_done"], c + 1)
                            act(mhi[:, c], mg[:, c], name="m_hi")
                    assert hi_next[0] == T_O + 2, hi_next

                    def ahead(i, e, c0, rate, length, u0, ts0, off=1024):
                        count = (i + (u0 // 2 + e)) * 16
                        for j in range(2):
                            hi((e + 1) % 2, (ts0 + 2 * e + 2 + j) % 4, length, count if j == 0 else None,
                               (i * (2 * rate) + (c0 + rate * e)) if j == 0 else None, j * off)

                    for i in range(UNITS_O):
                        ahead(i // 2, i % 2, N_O, 2, 1024, T_O // 2, T_O)
                        for j in range(2 * i, 2 * i + 2):
                            a.wait_ge(s["acc_out"], N_O + j + 1)
                            act(xhi[:, j], x[:, j], name="xhi_done", scale=par_("gffn", j))

                    def ffn_in(n0, t0, count, before, next_len, first_half):
                        def unit(i, e, length):
                            if isinstance(i, int) and i == 0 and e == 0 and first_half:
                                ahead(i, e, n0, 2, length, t0 // 2, t0, length if length < 1024 else 1024)
                                a.wait_ge(s["ss_mm"], 2)
                                rsqrt(halves(rstd[:]), m_halves(0), 1.0 / D_MODEL, RMS_EPS, "rstd_ln", "rstd_done")
                            else:
                                ahead(i, e, n0, 2, length, t0 // 2, t0, length if length < 1024 else 1024)
                            j = i * 2 + (e + before + 1)
                            a.wait_ge(s["acc_out"], i * 4 + (n0 + 2 * e + 1))
                            nc.scalar.activation(gt[:, 2 * e + 1], gt[:, 2 * e], ACT.Exp, scale=-1.0)\
                                .then_inc(s["h_x"], 1)
                            a.wait_ge(s["h_x"], j)
                            nc.scalar.activation(gt[:, 2 * e + 1], gt[:, 2 * e + 1], ACT.Ln, bias=1.0)\
                                .then_inc(s["h_r"], 1)
                            a.wait_ge(s["h_r"], j)
                            nc.scalar.activation(gt[:, 2 * e + 1], gt[:, 2 * e + 1], ACT.Exp, scale=-1.0)\
                                .then_inc(s["h_e"], 1)
                            a.wait_ge(s["h_h"], j)
                            nc.scalar.activation(column(hhi, i * 2 + e), gt[:, 2 * e], ACT.Copy).then_inc(s["h_hi"], 1)
                        pairs = count // 2
                        for e in range(2):
                            unit(0, e, 1024)
                        with a.Fori(1, pairs - 1) as i:
                            for e in range(2):
                                unit(i, e, 1024)
                        unit(pairs - 1, 0, 1024)
                        unit(pairs - 1, 1, next_len)

                    def ffn_out(n0, t0, count, last):
                        length = count // 2 * P
                        if not last:
                            with a.Fori(0, KD // 2 - 1) as i:
                                for e in range(2):
                                    ahead(i, e, n0, 1, length, t0 // 2, t0, length)
                            ahead(KD // 2 - 1, 0, n0, 1, length, t0 // 2, t0, length)
                            ahead(KD // 2 - 1, 1, n0, 1, 1024, t0 // 2, t0)
                            return
                        a.wait_ge(s["gm_in"], 16)
                        for j in range(KD):
                            off = length if j < KD - 1 else 1024
                            ahead(j // 2, j % 2, n0, 1, off, t0 // 2, t0, off)
                            a.wait_ge(s["acc_out"], n0 + j + 1)
                            a.dma_start(yt[:, j], x[:, j]).then_inc(y_out, 16)
                            act(xhi[:, j], x[:, j], name="xhi_done", scale=gmix[:, j:j + 1])
                    ffn_in(N_F1A, T_F1A, FA, 0, FA // 2 * P, True)
                    ffn_out(N_F2A, T_F2A, FA, False)
                    ffn_in(N_F1B, T_F1B, FB, FA, FB // 2 * P, False)
                    ffn_out(N_F2B, T_F2B, FB, True)
                    for name, value in (("cf_out", 32), ("sc_out", 32), ("kv_out", 64), ("s0_out", 32),
                                        ("sh_out", 16), ("x_in", 16)):
                        a.wait_ge(s[name], value)

                @block.vector
                def _(dve):
                    st = Steps(dve, "vec_order")

                    def tt(out, in0, in1, op, name=None):
                        return st(nc.vector.tensor_tensor(out, in0, in1, op), name)

                    def stt(out, in0, scalar, in1, op0, op1, name=None):
                        return st(nc.vector.scalar_tensor_tensor(out=out, in0=in0, scalar=scalar, in1=in1, op0=op0,
                                                                 op1=op1), name)

                    def lo(e, ts, length, t, off=0):
                        dve.wait_ge(s["hi_done"], t - 1)
                        nc.vector.tensor_tensor(wlo[:, ts, 0:length], raw[:, e, off:off + length],
                                                whi[:, ts, 0:length].bitcast(F32), ALU.subtract)\
                            .then_inc(s["lo_done"], 1)

                    def mix_lo(t):
                        lo((t // 2) % 2, t % 4, TILE_LEN[t], t, (t % 2) * 1024)

                    def x_lo(k, gain, count):
                        dve.wait_ge(s["xhi_done"], count)
                        stt(xlo[:, k], x[:, k], gain, xhi[:, k].bitcast(F32), ALU.mult, ALU.subtract,
                            "xlo_done")

                    def split(out, in_, hi_, name, ready):
                        dve.wait_ge(s[ready[0]], ready[1])
                        tt(out, in_, hi_.bitcast(F32), ALU.subtract, name)

                    def out_of(n, dst, name="acc_out"):
                        dve.wait_ge(s["acc_done"], n + 1)
                        return tt(halves(dst), acc_of(n % 2), halves(rstd[:]), ALU.mult, "acc_out")

                    dve.wait_ge(cst_in, 48)
                    zero = [st(nc.vector.memset(cfu[:, :, 0:W2 - 1], 0.0))]
                    lo_next = [2]
                    tap = [0]
                    tap_points = {}
                    written = {}
                    exp_index, exp_at = {}, {}
                    for n, (kind, c) in enumerate(SLOTS):
                        if kind in ("cfb", "gg") or (isinstance(kind, tuple) and kind[0] == "gate"):
                            exp_index[n] = len(exp_index) + 1
                            exp_at[kind, c] = exp_index[n]
                    adds = [0]

                    def gla_tmp(p):
                        return (tmp[:, 2], ge[:]) if p == 0 else (tmp[:, 0], tmp[:, 1])

                    def side(n):
                        if n == 4:
                            dve.wait_ge(s["par_in"], 16)
                        if SLOTS[n - 1][0] == "scb":
                            c = SLOTS[n - 1][1]
                            split(olo[0][:, c], sct[:, c % 2], ohi[0][:, c], "o_split", ("o_hi", c + 1))
                        if SLOTS[n - 1][0] == "gg":
                            c = SLOTS[n - 1][1]
                            dve.wait_ge(s["e_done"], exp_index[n - 1])
                            tt(gg[:, c], gg[:, c], tmp[:, c % 2], ALU.mult, "gg_done")
                        c = n - (S_AQ + 4)
                        if 0 <= c < 5:
                            v = q[:, c] if c < GROUP else kt[:]
                            dve.wait_ge(s["qk_r"], c + 1)
                            if c:
                                st.need(("qk_out", c))
                            r1 = tt(halves(gt[:, 2]), m_halves(2), halves(sinm), ALU.mult, "qk_rot")
                            r2 = tt(v, v, cosm, ALU.mult)
                            st.need(r1, r2)
                            tt(v, v, gt[:, 2], ALU.add, "qk_out")
                        c = n - (S_AQ + 2)
                        if 0 <= c < 5:
                            v = q[:, c] if c < GROUP else kt[:]
                            dve.wait_ge(s["qk_rn"], c + 1)
                            stt(v, v, par_("qn" if c < GROUP else "kn"), gt[:, 1], ALU.mult, ALU.mult, "qk_n")
                        if n == SATT:
                            st.need(("qk_out", 5))
                            dve.wait_ge(s["kts_in"], 16)
                            dve.wait_ge(s["qz_zero"], 1)
                            st(nc.vector.tensor_copy(kts[:, :, WIN - 1], kt[:, SEQ:T]))
                            for kv in range(NKV):
                                r = slice(kv * HEAD, kv * HEAD + HEAD)
                                st(nc.vector.tensor_copy(qz[r, :, kv * GROUP:kv * GROUP + GROUP], 
                                                         q[r, :, SEQ:T].rearrange("p g b -> p b g")),
                                   "s_q" if kv else None)
                        if n == SATT + 1:
                            dve.wait_ge(s["s_scores"], 1)
                            st.need(st(nc.vector.tensor_scalar(sprob[:], m4[0:NQ, 0, 0:P], HEAD ** -0.5, None,
                                                               ALU.mult)))
                            st.need(st(nc.vector.reduce_max(smax, sprob[:], AX)))
                            st.need(tt(smax, smax, par_("sink64", rows=NQ), ALU.max))
                            st(nc.vector.tensor_scalar(snmax, smax, -1.0, None, ALU.mult), "s_sub")
                        if n == SATT + 2:
                            dve.wait_ge(s["s_exp"], 1)
                            st.need(tt(slsum, slsum, sesink, ALU.add))
                            st.need(st(nc.vector.reciprocal(srl, slsum)))
                            st(nc.vector.tensor_scalar(sprob[:], sprob[:], srl, None, ALU.mult), "s_p")
                        if n == SATT + 3:
                            dve.wait_ge(s["s_t"], 1)
                            st(nc.vector.tensor_copy(pts.rearrange("p b h -> p (b h)"), m4[:, 2, 0:NS * NS]), "s_tc")
                        if n == SATT + 4:
                            dve.wait_ge(s["s_pv"], 1)
                            for kv in range(NKV):
                                r = slice(kv * HEAD, kv * HEAD + HEAD)
                                o = m4[r, 3, 0:NS * NS].rearrange("p (b v g) -> p v g b", b=NS, v=NKV)
                                st(nc.vector.tensor_copy(q[r, :, SEQ:T], o[:, kv]), "s_out")
                        for g in range(NBLK * NKV):
                            blk, kv = g // NKV, g % NKV
                            w = slice(0 if blk else P, 2 * P)
                            width = w.stop - w.start
                            if n == ATT[g] + 1:
                                dve.wait_ge(s["a_s"], g + 1)
                                if g:
                                    dve.wait_ge(s["a_t"], g)
                                else:
                                    dve.wait_ge(s["s_t"], 1)
                                mask = cst_("amask")[:, w].unsqueeze(1).broadcast_to([P, 2, width])
                                for b in range(2):
                                    sc_ = m4[:, b].rearrange("p (h n) -> p h n", h=2)[:, :, w]
                                    r = stt(prob[:, 2 * b:2 * b + 2, w], sc_, HEAD ** -0.5, mask, ALU.mult, ALU.add)
                                st.need(r)
                                st.need(st(nc.vector.reduce_max(rmax, prob[:, :, w], AX)))
                                st.need(tt(rmax, rmax, par_("sink", kv * GROUP, GROUP), ALU.max))
                                tt(esink, par_("sink", kv * GROUP, GROUP), rmax, ALU.subtract)
                                st(nc.vector.tensor_scalar(nmax, rmax, -1.0, None, ALU.mult), "a_max")
                            if n == ATT[g] + 2:
                                dve.wait_ge(s["a_exp"], g + 1)
                                st.need(tt(lsum, lsum, esink, ALU.add))
                                st.need(st(nc.vector.reciprocal(rl, lsum)))
                                tt(prob[:, :, w], prob[:, :, w], rl.unsqueeze(2).broadcast_to([P, GROUP, width]),
                                   ALU.mult, "a_p")
                        c = n - (ATT[-1] + 5)
                        if 0 <= c < KB:
                            split(olo[1][:, c], q[:, c], ohi[1][:, c], "o_split", ("o_hi", 4 + c + 1))
                        for p in range(2):
                            za, ze = gla_tmp(p)
                            if n == G_Z + 1 + 2 * p:
                                dve.wait_ge(s["g_z"], 1)
                                st.need(st(nc.vector.tensor_scalar(halves(za), m_halves(2 * p), par_("bg", p), None,
                                                                   ALU.add)))
                                stt(ze, za, -1.0, za, ALU.mult, ALU.min, "g_abs")
                                dve.wait_ge(s["g_log"], p + 1)
                                st.need(stt(za, za, 0.0, ze, ALU.min, ALU.subtract))
                                st(nc.vector.tensor_tensor_scan(out=gb[:, p], data0=scanm[:], data1=za, initial=0.0,
                                                                op0=ALU.mult, op1=ALU.add), "g_scan")
                            if n == G_Z + 2 + 2 * p:
                                dve.wait_ge(s["g_e1"], p + 1)
                                stt(gq[:, p, 0:SEQ], gq[:, p, 0:SEQ], HEAD ** -0.5, ze[:, 0:SEQ], ALU.mult, ALU.mult)
                                st(nc.vector.tensor_scalar(gq[:, p, SEQ:T], gq[:, p, SEQ:T], HEAD ** -0.5, None,
                                                           ALU.mult))
                                st(nc.vector.tensor_copy(gdec[p], ze[:, CHUNK - 1:SEQ:CHUNK]))
                                st(nc.vector.tensor_copy(gdecs[p], ze[:, SEQ:T]))
                                st.settled()
                                b3 = gb[:, p, 0:SEQ].rearrange("p (c n) -> p c n", c=NCHUNK)
                                tt(ze[:, 0:SEQ].rearrange("p (c n) -> p c n", c=NCHUNK),
                                   b3[:, :, CHUNK - 1:CHUNK].broadcast_to([P, NCHUNK, CHUNK]), b3, ALU.subtract,
                                   "g_gap")
                                dve.wait_ge(s["g_e3"], p + 1)
                                dve.wait_ge(s["g_e2"], p + 1)
                                st.need(("g_gap", p + 1))
                                tt(gb[:, p, 0:SEQ], gk[:, p, 0:SEQ], ze[:, 0:SEQ], ALU.mult)
                                r = st(nc.vector.tensor_copy(gb[:, p, SEQ:T], gk[:, p, SEQ:T]))
                                st.need(r)
                                tt(gk[:, p, 0:SEQ], gk[:, p, 0:SEQ], za[:, 0:SEQ], ALU.mult, "g_prep")
                        if n == G_U:
                            st(nc.vector.memset(am[:], 0.0))
                        if n == G_U + 1:
                            dve.wait_ge(s["g_u"], 1)
                            last = [None, None]
                            for c in range(NCHUNK):
                                for p in range(2):
                                    o = ((c // 2) % 2) * 256 + p * P
                                    u = m4[:, (c % 2) * 2 + c // 4, o:o + P]
                                    end = c == NCHUNK - 1 and p == 1
                                    if c == 0:
                                        last[p] = st(nc.vector.tensor_copy(sh[:, 0, p], u))
                                    else:
                                        st.need(last[p])
                                        last[p] = stt(sh[:, c, p], sh[:, c - 1, p], gdec[p][:, c:c + 1], u, ALU.mult,
                                                      ALU.add, "g_state" if end else None)
                        if n == LN_CONV:
                            dve.wait_ge(s["conv_in"], 32)
                            for c in range(KB):
                                w = par_("cc", c * W2, W2).unsqueeze(1).broadcast_to([P, NS, W2])
                                prod = tmp[:, c % 2, 0:NS * W2].rearrange("p (b w) -> p b w", b=NS)
                                st.need(tt(prod, cfs[:, c], w, ALU.mult))
                                st.need(st(nc.vector.reduce_sum(cacc[:, c, SEQ:T], prod, AX)))
                                st(nc.vector.tensor_scalar(cacc[:, c, SEQ:T], cacc[:, c, SEQ:T], par_("ccb", c), None,
                                                           ALU.add))
                        if n == LN_XC:
                            dve.wait_ge(s["ln_sum"], 1)
                            for c in range(KB):
                                stt(halves(cacc[:, c]), m_halves(0), -1.0 / BW, halves(cacc[:, c]), ALU.mult, ALU.add,
                                    "ln_xc" if c == KB - 1 else None)
                        c = n - LN_Y
                        if 0 <= c < KB:
                            dve.wait_ge(s["ln_r"], 1)
                            st.need(stt(cacc[:, c], cacc[:, c], par_("lng", c), tmp[:, 0], ALU.mult, ALU.mult))
                            st(nc.vector.tensor_scalar(cacc[:, c], cacc[:, c], par_("lnb", c), None, ALU.add), "ln_y")
                        c = n - (LN_Y + 2)
                        if 0 <= c < KB:
                            dve.wait_ge(s["ln_e"], c + 1)
                            tt(cacc[:, c], cacc[:, c], cfu[:, c, 0:T], ALU.mult, "ln_o")
                        for b in range(NBLK):
                            if n == G_A[b] + 1:
                                dve.wait_ge(s["ga_a"], b + 1)
                                if b:
                                    dve.wait_ge(s["ga_o"], b)
                                for hh in range(2):
                                    for p in range(2):
                                        st(nc.vector.copy_predicated(am[:, 2 * hh + p], glam[:],
                                                                     m4[:, hh, p * P:p * P + P]),
                                           "ga_m" if hh and p else None)
                        c = n - S_GATE_B
                        if 0 <= c < KB:
                            split(olo[1][:, c], cacc[:, c], ohi[1][:, c], "o_split", ("o_hi", 8 + c + 1))
                        for p in range(2):
                            if n == G_S[p] - (1 - p):
                                if p == 0:
                                    dve.wait_ge(s["ga_o"], NBLK)
                                    dve.wait_ge(s["gqz_zero"], 1)
                                    for pp in range(2):
                                        for hh in range(2):
                                            r = slice(hh * HEAD, hh * HEAD + HEAD)
                                            st(nc.vector.tensor_copy(gqz[r, pp, :, hh], gq[r, pp, SEQ:T]),
                                               "gqz_done" if pp and hh else None)
                                else:
                                    dve.wait_ge(s["gs_mm"], 1)
                                eye = cst_("eye8", NS).unsqueeze(2).broadcast_to([NS, NS, P])
                                for hh in range(2):
                                    h = 2 * p + hh
                                    tt(vbd[hh][:], vst[:, h * P:h * P + P].unsqueeze(1).broadcast_to([NS, NS, P]), eye,
                                       ALU.mult, "gs_v" if hh else None)
                            if n == G_S[p] + 1:
                                dve.wait_ge(s["gs_mm"], p + 1)
                                for b in range(NS):
                                    stt(s0[p][:, b], s0[p][:, b], gdecs[p][:, b:b + 1],
                                        m4[:, b // 4, (b % 4) * P:(b % 4) * P + P], ALU.mult, ALU.add,
                                        "gs_s" if b == NS - 1 else None)
                            if n == G_S[p] + 3:
                                dve.wait_ge(s["gs_t"], p + 1)
                                o = m4[:, 3, 0:2 * NS].rearrange("p (b h) -> p h b", b=NS)
                                st(nc.vector.tensor_copy(gv[:, 2 * p:2 * p + 2, SEQ:T], o), "gs_g")
                        h = n - (G_N + 1)
                        if 0 <= h < 4:
                            dve.wait_ge(s["gn_r"], h + 1)
                            st.need(stt(gv[:, h], gv[:, h], par_("gn"), ge[:], ALU.mult, ALU.mult))
                            st.need(("gg_done", 4))
                            tt(gv[:, h], gv[:, h], gg[:, h], ALU.mult, "gn_o")
                        h = n - (G_N + 2)
                        if 0 <= h < 4:
                            split(olo[0][:, h], gv[:, h], ohi[0][:, h], "o_split", ("o_hi", 12 + h + 1))

                    def evac(n, kind, c):
                        gate = isinstance(kind, tuple) and kind[0] == "gate"
                        branch = isinstance(kind, tuple) and kind[0] == "branch"
                        if n == 0:
                            dve.wait_ge(s["rstd_done"], 1)
                        if kind == "cfb":
                            out_of(n, gt[:, c % 2])
                        elif kind == "cfa":
                            r = out_of(n, gt[:, 2 + c % 2])
                            st.need(r)
                            dve.wait_ge(s["e_done"], exp_at["cfb", c])
                            dve.wait_ge(s["conv_in"], 32)
                            u = tt(cfs[:, c, :, W2 - 1], gt[:, 2 + c % 2, SEQ:T], gt[:, c % 2, SEQ:T], ALU.mult)
                            written[("cfu", c)] = tt(cfu[:, c, W2 - 1:W2 - 1 + SEQ], gt[:, 2 + c % 2, 0:SEQ],
                                                     gt[:, c % 2, 0:SEQ], ALU.mult, "cf_written")
                        elif kind == "aq":
                            out_of(n, q[:, c])
                        elif kind == "ak":
                            out_of(n, kt[:])
                        elif kind == "av":
                            out_of(n, vt[:])
                        elif kind == "sch":
                            if n == S_SCH:
                                zero.append(st(nc.vector.memset(scu[:, :, 0:W1 - 1], 0.0)))
                            if c >= 2:
                                st.need(("o_split", c - 1))
                            out_of(n, sct[:, c % 2])
                        elif kind == "scc":
                            y = sct[:, c % 2]
                            st.need(out_of(n, tmp[:, c % 2]))
                            tt(scs[:, c, :, W1 - 1], tmp[:, c % 2, SEQ:T], y[:, SEQ:T], ALU.mult)
                            st.need(tt(scu[:, c, W1 - 1:W1 - 1 + SEQ], tmp[:, c % 2, 0:SEQ], y[:, 0:SEQ], ALU.mult,
                                       "sc_written"))
                            w = [par_("cs", c * W1 + i) for i in range(W1)]
                            for i in range(W1):
                                up, us = scu[:, c, i:i + SEQ], scs[:, c, :, i]
                                if i == 0:
                                    st(nc.vector.tensor_scalar(y[:, 0:SEQ], up, w[0], None, ALU.mult))
                                    st(nc.vector.tensor_scalar(y[:, SEQ:T], us, w[0], None, ALU.mult))
                                else:
                                    st.settled()
                                    stt(y[:, 0:SEQ], up, w[i], y[:, 0:SEQ], ALU.mult, ALU.add)
                                    stt(y[:, SEQ:T], us, w[i], y[:, SEQ:T], ALU.mult, ALU.add)
                            st.settled()
                        elif kind == "scb":
                            y = sct[:, c % 2]
                            st.need(out_of(n, tmp[:, c % 2]))
                            tt(y, y, tmp[:, c % 2], ALU.mult, "sc_o")
                        elif kind == "gq":
                            if c == 0:
                                dve.wait_ge(s["kv_out"], 64)
                            out_of(n, gq[:, c])
                        elif kind == "gk":
                            out_of(n, gk[:, c])
                        elif kind == "gv":
                            out_of(n, gv[:, c])
                        elif kind == "ga":
                            out_of(n, tmp[:, 2])
                        elif kind == "gg":
                            out_of(n, gg[:, c])
                        elif gate:
                            if adds[0]:
                                dve.wait_ge(s["add_done"], adds[0] - 3 + c % 4)
                            out_of(n, gt[:, c % 4])
                        elif branch:
                            i = c % 4
                            dve.wait_ge(s["acc_done"], n + 1)
                            dve.wait_ge(s["e_done"], exp_at[("gate", kind[1]), c])
                            if kind[1] == 0:
                                if c == 0:
                                    dve.wait_ge(s["sc_out"], 32)
                                tt(halves(mg[:, c]), acc_of(n % 2), halves(gt[:, i]), ALU.mult, "acc_out")
                            else:
                                r = tt(halves(gt[:, i]), acc_of(n % 2), halves(gt[:, i]), ALU.mult, "acc_out")
                                if kind[1] == 3:
                                    st.need(r)
                                    if c == 0:
                                        dve.wait_ge(s["add_done"], 2 * KD)
                                    tt(mg[:, c], mg[:, c], gt[:, i], ALU.add, "mg_done")
                                    if c == 0:
                                        dve.wait_ge(s["s0_out"], 32)
                                        dve.wait_ge(s["sh_out"], 16)
                                    for k in ([c - 1] if c else []) + ([c] if c == KD - 1 else []):
                                        split(mlo[:, k], mg[:, k], mhi[:, k], "m_split", ("m_hi", k + 1))
                                else:
                                    adds[0] += 1

                    for n, (kind, c) in enumerate(SLOTS):
                        if n not in LO_FIRST:
                            side(n)
                        while lo_next[0] <= last_tile(n + 2):
                            mix_lo(lo_next[0])
                            lo_next[0] += 1
                        if n in LO_FIRST:
                            side(n)
                        evac(n, kind, c)
                        for _ in range(TAPS_AT.get(n, 0)):
                            tc_, tw = TAPS[tap[0]]
                            src = cfu[:, tc_, tw:tw + SEQ]
                            w = par_("cc", tc_ * W2 + tw)
                            if tw == 0:
                                st.need(written[("cfu", tc_)], zero[0])
                                r = st(nc.vector.tensor_scalar(cacc[:, tc_, 0:SEQ], src, w, par_("ccb", tc_), ALU.mult,
                                                               ALU.add))
                            else:
                                st.need(tap_points[tc_])
                                r = stt(cacc[:, tc_, 0:SEQ], src, w, cacc[:, tc_, 0:SEQ], ALU.mult, ALU.add,
                                        "conv_done" if tap[0] == len(TAPS) - 1 else None)
                            tap_points[tc_] = r
                            tap[0] += 1
                    assert lo_next[0] == T_O + 2 and tap[0] == len(TAPS)

                    def ahead(i, e, length, t0, j, off=1024):
                        lo((e + 1) % 2, (t0 + 2 * e + 2 + j) % 4, length, i * 4 + (t0 + 2 * e + 2 + j), j * off)

                    dve.wait_ge(s["x_in"], 16)
                    for j in range(KD):
                        ahead(j // 4, (j // 2) % 2, 1024, T_O, j % 2)
                        dve.wait_ge(s["acc_done"], N_O + j + 1)
                        tt(halves(x[:, j]), halves(x[:, j]), acc_of(j % 2), ALU.add, "acc_out")
                        x_lo(j, par_("gffn", j), j + 1)

                    def ffn_in(n0, t0, count, before, next_len, first_half):
                        def unit(i, e, length):
                            off = length if length < 1024 else 1024
                            j = i * 2 + (e + before + 1)
                            t, r = gt[:, 2 * e], gt[:, 2 * e + 1]
                            if isinstance(i, int) and i == 0 and e == 0 and first_half:
                                dve.wait_ge(s["rstd_done"], 2)
                            dve.wait_ge(s["acc_done"], i * 4 + (n0 + 2 * e + 1))
                            if before or not (isinstance(i, int) and i == 0):
                                dve.wait_ge(s["h_lo"], i * 2 + (e + before - 1))
                            nc.vector.tensor_tensor(halves(t), acc_of(0), halves(rstd[:]), ALU.mult)\
                                .then_inc(s["acc_out"], 1)
                            ahead(i, e, length, t0, 0, off)
                            dve.wait_ge(s["h_e"], j)
                            nc.vector.tensor_tensor(t, t, r, ALU.mult).then_inc(s["h_t"], 1)
                            ahead(i, e, length, t0, 1, off)
                            dve.wait_ge(s["acc_done"], i * 4 + (n0 + 2 * e + 2))
                            dve.wait_ge(s["h_t"], j)
                            nc.vector.tensor_tensor(halves(r), acc_of(1), halves(rstd[:]), ALU.mult)\
                                .then_inc(s["acc_out"], 1)
                            dve.wait_ge(s["acc_out"], i * 4 + (n0 + 2 * e + 2))
                            nc.vector.tensor_tensor(t, t, r, ALU.mult).then_inc(s["h_h"], 1)
                            dve.wait_ge(s["h_hi"], j)
                            nc.vector.tensor_tensor(column(hlo, i * 2 + e), t, column(hhi, i * 2 + e).bitcast(F32),
                                                    ALU.subtract).then_inc(s["h_lo"], 1)
                        pairs = count // 2
                        for e in range(2):
                            unit(0, e, 1024)
                        with dve.Fori(1, pairs - 1) as i:
                            for e in range(2):
                                unit(i, e, 1024)
                        unit(pairs - 1, 0, 1024)
                        unit(pairs - 1, 1, next_len)

                    def ffn_out(n0, t0, count, last):
                        length = count // 2 * P

                        def chunk(i, e, length, off):
                            for j in range(2):
                                ahead(i, e, length, t0, j, off)
                            dve.wait_ge(s["acc_done"], i * 2 + (n0 + e + 1))
                            xj = column(x, i * 2 + e)
                            nc.vector.tensor_tensor(halves(xj), halves(xj), acc_of(e), ALU.add)\
                                .then_inc(s["acc_out"], 1)
                        if not last:
                            with dve.Fori(0, KD // 2 - 1) as i:
                                for e in range(2):
                                    chunk(i, e, length, length)
                            chunk(KD // 2 - 1, 0, length, length)
                            chunk(KD // 2 - 1, 1, 1024, 1024)
                            return
                        dve.wait_ge(s["gm_in"], 16)
                        for j in range(KD):
                            off = length if j < KD - 1 else 1024
                            chunk(j // 2, j % 2, off, off)
                            if j:
                                x_lo(j - 1, gmix[:, j - 1:j], KD + j)
                        x_lo(KD - 1, gmix[:, KD - 1:KD], 2 * KD)
                    ffn_in(N_F1A, T_F1A, FA, 0, FA // 2 * P, True)
                    ffn_out(N_F2A, T_F2A, FA, False)
                    ffn_in(N_F1B, T_F1B, FB, FA, FB // 2 * P, False)
                    ffn_out(N_F2B, T_F2B, FB, True)

                @block.gpsimd
                def _(g):
                    st = Steps(g, "pool_order")
                    g.wait_ge(s["vs_in"], 16)
                    nc.gpsimd.memset(qz[:], 0.0).then_inc(s["qz_zero"], 1)
                    g.wait_ge(s["cf_written"], KB)
                    g.wait_ge(s["ss_mm"], 1)
                    g.wait_ge(s["par_in"], 16)
                    c = KB - 1
                    st(nc.gpsimd.tensor_scalar(cacc[:, c, 0:SEQ], cfu[:, c, 0:SEQ], par_("cc", c * W2), par_("ccb", c),
                                               ALU.mult, ALU.add))
                    for w in range(1, W2):
                        st.settled()
                        st(nc.gpsimd.tensor_scalar(ssum[:, 0:SEQ], cfu[:, c, w:w + SEQ], par_("cc", c * W2 + w), None,
                                                   ALU.mult))
                        st.settled()
                        st(nc.gpsimd.tensor_tensor(cacc[:, c, 0:SEQ], cacc[:, c, 0:SEQ], ssum[:, 0:SEQ], ALU.add),
                           None)

                    def add_chunks(of_chunk):
                        for c in range(1, KB):
                            tgt = ssum[:] if c > 1 else of_chunk(0)
                            st(nc.gpsimd.tensor_tensor(ssum[:], tgt, of_chunk(c), ALU.add),
                               "ln_add" if c == KB - 1 else None)
                            if c < KB - 1:
                                st.settled()
                    g.wait_ge(s["conv_done"], 1)
                    st.settled()
                    add_chunks(lambda c: cacc[:, c])
                    for n, (kind, c) in enumerate(SLOTS):
                        if n == LN_XC + 1:
                            g.wait_ge(s["ln_sq"], 1)
                            g.wait_ge(s["ln_sum"], 1)
                            add_chunks(lambda c: cfu[:, c, 0:T])
                        if kind in (("branch", 2), ("branch", 1)):
                            g.wait_ge(s["acc_out"], n + 1)
                            st(nc.gpsimd.tensor_tensor(mg[:, c], mg[:, c], gt[:, c % 4], ALU.add), "add_done")
                        if n == LN_Y + KB + 2:
                            g.wait_ge(s["ln_o"], KB)
                            nc.gpsimd.memset(gqz[:], 0.0).then_inc(s["gqz_zero"], 1)

                    def square_add(g, xj, e, done):
                        nc.gpsimd.tensor_tensor(tmp[:, e], xj, xj, ALU.mult).then_inc(s["ss_sq"], 1)
                        g.wait_ge(s["ss_sq"], done + 1)
                        g.wait_ge(s["ss_done"], done)
                        nc.gpsimd.tensor_tensor(ssum[:], ssum[:], tmp[:, e], ALU.add).then_inc(s["ss_done"], 1)
                    for j in range(KD):
                        g.wait_ge(s["acc_out"], N_O + j + 1)
                        if j == 0:
                            nc.gpsimd.tensor_tensor(tmp[:, 0], x[:, 0], x[:, 0], ALU.mult).then_inc(s["ss_sq"], 1)
                            g.wait_ge(s["ss_sq"], 1)
                            nc.gpsimd.tensor_copy(ssum[:], tmp[:, 0]).then_inc(s["ss_done"], 1)
                        else:
                            square_add(g, x[:, j], j % 2, j)
                    g.wait_ge(s["acc_out"], N_F2B + 1)
                    nc.gpsimd.tensor_tensor(tmp[:, 0], x[:, 0], x[:, 0], ALU.mult).then_inc(s["ss_sq"], 1)
                    g.wait_ge(s["ss_sq"], KD + 1)
                    nc.gpsimd.tensor_copy(ssum[:], tmp[:, 0]).then_inc(s["ss_done"], 1)
                    g.wait_ge(s["acc_out"], N_F2B + 2)
                    square_add(g, x[:, 1], 1, KD + 1)
                    with g.Fori(1, KD // 2) as i:
                        for e in range(2):
                            g.wait_ge(s["acc_out"], i * 2 + (N_F2B + e + 1))
                            square_add(g, column(x, i * 2 + e), e, i * 2 + (KD + e))
            nc.all_engine_barrier(sems_to_clear=range(first_sem.num, last_sem.num + 1))
        with nc.Block() as block:
            @block.sync
            def _(sp):
                sp.wait_ge(y_out, DEPTH * KD * 16 + 16)


def lay_out(inputs):
    f = {k: np.asarray(v) for k, v in inputs.items()}
    w_in, w_br, w_out = f["w_in"], f["w_branch"], f["w_out"]
    w1, w2 = f["w_ffn_in"], f["w_ffn_out"]
    wt = np.zeros((DEPTH * UNITS + 2, P, 2048), np.float32)
    wl = wt[:DEPTH * UNITS].reshape(DEPTH, UNITS, P, 2048)
    qcols = [C_AQ + np.concatenate([g * HEAD + np.arange(HEAD), (GROUP + g) * HEAD + np.arange(HEAD)])
             for g in range(GROUP)]
    start = {"sch": C_SCH, "scb": C_SCB, "scc": C_SCC, "cfa": C_CFA, "cfb": C_CFB, "ak": C_AK, "av": C_AV,
             "gq": C_GQ, "gk": C_GK, "gv": C_GV, "gg": C_GG, "ga": C_GA}
    rows_c = np.concatenate(qcols) - C_AQ

    def tile(w, cols, k0, k1):
        return w[k0 * P:k1 * P][:, cols].reshape(k1 - k0, P, P).transpose(1, 0, 2).reshape(P, -1)
    for l in range(DEPTH):
        tiles = np.zeros((UNITS * 2, P, 1024), np.float32)
        for (kind, c), (ts, off) in zip(SLOTS, TILE_OF):
            if isinstance(kind, tuple) and kind[0] == "branch":
                w = w_br[l, kind[1]]
                if kind[1] == 2:
                    w = w[rows_c]
                tiles[ts[0]][:, off:off + KB * P] = tile(w, slice(c * P, c * P + P), 0, KB)
                continue
            if isinstance(kind, tuple):
                cols = slice(C_GATE + kind[1] * D_MODEL + c * P, C_GATE + kind[1] * D_MODEL + c * P + P)
            elif kind == "aq":
                cols = qcols[c]
            else:
                cols = slice(start[kind] + c * P, start[kind] + c * P + P)
            n = KD // len(ts)
            for i, t in enumerate(ts):
                tiles[t][:, 0:n * P] = tile(w_in[l], cols, n * i, n * i + n)
        for j in range(KD):
            tiles[T_O + j] = tile(w_out[l], slice(j * P, j * P + P), 0, KD)
        for t0, c0, n in ((T_F1A, 0, FA), (T_F1B, FA, FB)):
            for j in range(n):
                for side in range(2):
                    a = side * D_FF + (c0 + j) * P
                    tiles[t0 + 2 * j + side] = tile(w1[l], slice(a, a + P), 0, KD)
        wl[l] = tiles.reshape(UNITS, 2, P, 1024).transpose(0, 2, 1, 3).reshape(UNITS, P, 2048)
        for t0, c0, n in ((T_F2A, 0, FA), (T_F2B, FA, FB)):
            for j in range(KD):
                wl[l, t0 // 2 + j][:, 0:n * P] = tile(w2[l], slice(j * P, j * P + P), c0, c0 + n)
    par = np.zeros((DEPTH, P, NPAR), np.float32)

    def put(name, v, rows=P):
        a, b = PAR[name]
        par[:, 0:rows, a:b] = v

    def cols(v, n):
        return v.reshape(DEPTH, n, P).transpose(0, 2, 1)
    put("gffn", cols(f["norm_ffn"], KD))
    put("cs", f["conv_short"].reshape(DEPTH, W1, KB, P).transpose(0, 3, 2, 1).reshape(DEPTH, P, -1))
    put("cc", f["conv_conf"].reshape(DEPTH, W2, KB, P).transpose(0, 3, 2, 1).reshape(DEPTH, P, -1))
    put("ccb", cols(f["conv_conf_b"], KB))
    put("lng", cols(f["conf_ln_g"], KB))
    put("lnb", cols(f["conf_ln_b"], KB))
    put("qn", np.tile(f["q_norm"], (1, NKV))[:, :, None])
    put("kn", np.tile(f["k_norm"], (1, NKV))[:, :, None])
    put("sink", np.broadcast_to(f["attn_sinks"][:, None, :], (DEPTH, P, NKV * GROUP)))
    put("sink64", np.tile(f["attn_sinks"], (1, NS))[:, :, None], NS * NKV * GROUP)
    put("bg", cols(f["b_gla_gate"], 2))
    put("gn", f["gla_norm"][:, :, None])
    put("wg", f["w_gla_gate"], 16)
    x = np.concatenate([f["x_prompt"][0], f["x_sample"][:, 0]], axis=0)
    xt = np.ascontiguousarray(x.T.reshape(KD, P, T).transpose(1, 0, 2))
    kc = f["cache_swa_k"][:, :, 1:].transpose(0, 3, 4, 1, 2).reshape(DEPTH, P, NS, WIN - 1)
    vc = f["cache_swa_v"][:, :, 1:].transpose(0, 2, 1, 3, 4).reshape(DEPTH, WIN - 1, NS, P)
    sc = f["state_sconv"].reshape(DEPTH, NS, 2, KB, P).transpose(0, 4, 3, 1, 2)
    cc = f["state_cconv"].reshape(DEPTH, NS, W2 - 1, KB, P).transpose(0, 4, 3, 1, 2)
    gs = f["state_gla"].reshape(DEPTH, NS, 2, P, P).transpose(0, 2, 3, 1, 4)
    cst, glam, scanm = constants()
    gm = np.zeros((DEPTH + 1, P, KD), np.float32)
    gm[:DEPTH] = cols(f["norm_mix"], KD)
    out = {"wt": wt, "xt": xt, "gm": gm, "par": par, "cst": cst, "glam": glam, "scan": scanm,
           "kc": kc, "vc": vc, "sc": sc,
           "cc": cc, "gs": gs}
    return {k: np.ascontiguousarray(v) for k, v in out.items()}


_OUTS = [("yt", (P, KD, T)), ("o_sc", (DEPTH, P, KB, W1 - 1)), ("o_scs", (DEPTH, P, KB, NS, W1 - 1)),
         ("o_cc", (DEPTH, P, KB, W2 - 1)), ("o_ccs", (DEPTH, P, KB, NS, W2 - 1)),
         ("o_k", (DEPTH, P, WIN)), ("o_ks", (DEPTH, P, NS, WIN)), ("o_v", (DEPTH, P, WIN)), ("o_vs", (DEPTH, P, NS, P)),
         ("o_g", (DEPTH, P, 2, P)), ("o_gs", (DEPTH, 2, P, NS, P))]


def kernel(**inputs):
    import concourse.bacc as bacc
    from concourse.bass_utils import run_bass_kernel_spmd
    arrays = lay_out(inputs)
    nc = bacc.Bacc("TRN2", target_bir_lowering=False, num_devices=1, dynamic_dma_scratch_size=1024)
    ins = [nc.dram_tensor("in_" + k, list(v.shape), mybir.dt.from_np(v.dtype), kind="ExternalInput").ap()
           for k, v in arrays.items()]
    outs = [nc.dram_tensor(k, list(shape), F32, kind="ExternalOutput").ap() for k, shape in _OUTS]
    build(nc, *ins, *outs)
    got = run_bass_kernel_spmd(nc, [{"in_" + k: v for k, v in arrays.items()}], core_ids=[0]).results[0]
    y = got["yt"].transpose(1, 0, 2).reshape(D_MODEL, T).T
    c = np.ascontiguousarray

    def channels(v, *axes):
        v = np.moveaxis(np.moveaxis(v, 2, -1), 1, -1)
        return v.reshape(*v.shape[:-2], BW)
    kh = got["o_k"].reshape(DEPTH, 1, NKV, HEAD, WIN).transpose(0, 1, 4, 2, 3)
    vh = got["o_v"].reshape(DEPTH, 1, NKV, HEAD, WIN).transpose(0, 1, 4, 2, 3)
    ks = got["o_ks"].reshape(DEPTH, NKV, HEAD, NS, WIN).transpose(0, 3, 4, 1, 2)
    vs = got["o_vs"].reshape(DEPTH, WIN, NS, NKV, HEAD).transpose(0, 2, 1, 3, 4)
    g = got["o_g"].reshape(DEPTH, 2, HEAD, 2, P).transpose(0, 3, 1, 2, 4).reshape(DEPTH, 1, 4, HEAD, P)
    gs = got["o_gs"].reshape(DEPTH, 2, 2, HEAD, NS, P).transpose(0, 4, 1, 2, 3, 5).reshape(DEPTH, NS, 4, HEAD, P)
    return (c(y[None, :SEQ]), c(y[SEQ:, None]),
            c(channels(got["o_sc"])[:, None]), c(channels(got["o_scs"])),
            c(channels(got["o_cc"])[:, None]), c(channels(got["o_ccs"])),
            c(kh), c(ks), c(vh), c(vs), c(g), c(gs))
```
